# Optimizing a Trainium2 kernel written in Bass

```python
import math
import jax, jax.numpy as jnp
from jax import lax
import numpy as np

D_MODEL = 1024
BATCH = 1
SEQ = 1024
DEPTH = 1

CHUNK = 64

MIX_WIDTH = D_MODEL
POOL_WIDTH = MIX_WIDTH // 2
POOL_WINDOWS = (2, 4, 8, 16)
POOL_GROUPS = len(POOL_WINDOWS)
POOL_GROUP_DIM = POOL_WIDTH // POOL_GROUPS
SB_WIDTH = MIX_WIDTH - POOL_WIDTH
SB_HEADS = 8
SB_HEAD_DIM = SB_WIDTH // SB_HEADS
Q_BLOCK = 128
IN_PROJ_WIDTH = POOL_WIDTH + 3 * SB_WIDTH

PEER_HEADS = 8
PEER_N_KEYS = 128
PEER_N_EXPERTS = PEER_N_KEYS * PEER_N_KEYS
PEER_TOPK = 16
PEER_KEY_DIM = 256
PEER_HALF_DIM = PEER_KEY_DIM // 2
PEER_TOKEN_BLOCK = 128

LN_EPS = 1e-5
DN_ALPHA = (2.0 * DEPTH) ** 0.25
DN_BETA = (8.0 * DEPTH) ** -0.25

kernel_name = "hybrid_pool_stickbreak_peer_deepnorm"

def layer_norm(x, g, b):
    xf = x.astype(jnp.float32)
    mu = jnp.mean(xf, axis=-1, keepdims=True)
    var = jnp.mean(jnp.square(xf - mu), axis=-1, keepdims=True)
    y = (xf - mu) * lax.rsqrt(var + LN_EPS) * g.astype(jnp.float32) + b.astype(jnp.float32)
    return y.astype(x.dtype)

def pool_mixer(u, pool_w, pool_b, pool_scale):
    B, S, _ = u.shape
    ug = u.reshape(B, S, POOL_GROUPS, POOL_GROUP_DIM).astype(jnp.float32)
    cs = jnp.cumsum(ug, axis=1)
    pos = jnp.arange(S)
    outs = []
    for g, w in enumerate(POOL_WINDOWS):
        c = cs[:, :, g]
        shifted = jnp.pad(c, ((0, 0), (w, 0), (0, 0)))[:, :S]
        count = jnp.minimum(pos + 1, w).astype(jnp.float32)[None, :, None]
        outs.append((c - shifted) / count - ug[:, :, g])
    pooled = jnp.stack(outs, axis=2).astype(u.dtype)
    mixed = jnp.einsum('bsgc,gcd->bsgd', pooled, pool_w) + pool_b
    return mixed.reshape(B, S, POOL_WIDTH) * pool_scale

def stick_breaking_attention(q, k, v):
    S = q.shape[2]
    scale = 1.0 / math.sqrt(SB_HEAD_DIM)
    outs = []
    for i in range(S // Q_BLOCK):
        q0 = i * Q_BLOCK
        kend = q0 + Q_BLOCK
        z = jnp.einsum('bhqd,bhkd->bhqk', q[:, :, q0:kend], k[:, :, :kend]).astype(jnp.float32) * scale
        t_idx = q0 + jnp.arange(Q_BLOCK)[:, None]
        s_idx = jnp.arange(kend)[None, :]
        mask = s_idx < t_idx
        log_1m_beta = jnp.where(mask, jax.nn.log_sigmoid(-z), 0.0)
        after = lax.cumsum(log_1m_beta, axis=3, reverse=True) - log_1m_beta
        a = jnp.where(mask, jnp.exp(jax.nn.log_sigmoid(z) + after), 0.0)
        outs.append(jnp.einsum('bhqk,bhkd->bhqd', a.astype(v.dtype), v[:, :, :kend]))
    return jnp.concatenate(outs, axis=2)

def hybrid_mixer(x, w_in, pool_w, pool_b, pool_scale, w_out):
    B, S, _ = x.shape
    h = x @ w_in
    u = h[..., :POOL_WIDTH]
    qkv = h[..., POOL_WIDTH:].reshape(B, S, 3, SB_HEADS, SB_HEAD_DIM)
    q = jnp.transpose(qkv[:, :, 0], (0, 2, 1, 3))
    k = jnp.transpose(qkv[:, :, 1], (0, 2, 1, 3))
    v = jnp.transpose(qkv[:, :, 2], (0, 2, 1, 3))
    a_out = pool_mixer(u, pool_w, pool_b, pool_scale)
    b_out = jnp.transpose(stick_breaking_attention(q, k, v), (0, 2, 1, 3)).reshape(B, S, SB_WIDTH)
    return jnp.concatenate([a_out, b_out], axis=-1) @ w_out

def peer(x, w_query, sub_keys, u_table, v_table):
    B, S, D = x.shape
    T = B * S
    xt = x.reshape(T, D)
    q = (xt @ w_query).reshape(T, PEER_HEADS, 2, PEER_HALF_DIM)
    scores = jnp.einsum('thpc,pnc->thpn', q, sub_keys).astype(jnp.float32)
    top_s, top_i = lax.top_k(scores, PEER_TOPK)
    cand_s = (top_s[:, :, 0, :, None] + top_s[:, :, 1, None, :]).reshape(T, PEER_HEADS, PEER_TOPK * PEER_TOPK)
    cand_i = (top_i[:, :, 0, :, None] * PEER_N_KEYS + top_i[:, :, 1, None, :]).reshape(T, PEER_HEADS, PEER_TOPK * PEER_TOPK)
    best_s, best_pos = lax.top_k(cand_s, PEER_TOPK)
    expert_idx = jnp.take_along_axis(cand_i, best_pos, axis=-1)
    gate = jax.nn.softmax(best_s, axis=-1).astype(x.dtype)

    n_blocks = T // PEER_TOKEN_BLOCK

    def block_fn(args):
        xb, idx, g = args
        u_sel = u_table[idx]
        hid = jnp.einsum('td,thkd->thk', xb, u_sel)
        act = jax.nn.gelu(hid, approximate=False) * g
        v_sel = v_table[idx]
        return jnp.einsum('thk,thkd->td', act, v_sel)

    out = lax.map(block_fn, (xt.reshape(n_blocks, PEER_TOKEN_BLOCK, D),
                             expert_idx.reshape(n_blocks, PEER_TOKEN_BLOCK, PEER_HEADS, PEER_TOPK),
                             gate.reshape(n_blocks, PEER_TOKEN_BLOCK, PEER_HEADS, PEER_TOPK)))
    return out.reshape(B, S, D)

def setup_inputs(seed: int = 0) -> dict:
    key = jax.random.key(seed)
    ks = jax.random.split(key, 20)
    f32 = jnp.float32
    L = DEPTH
    D = D_MODEL

    def nrm(k, shape, scale):
        return jax.random.normal(k, shape, f32) * scale

    x = jax.random.normal(ks[0], (BATCH, SEQ, D), f32)
    ln0_g = 1.0 + nrm(ks[1], (D,), 0.02)
    ln0_b = nrm(ks[2], (D,), 0.02)
    w_in_pqk = nrm(ks[3], (L, D, POOL_WIDTH + 2 * SB_WIDTH), D ** -0.5)
    w_in_v = nrm(ks[4], (L, D, SB_WIDTH), D ** -0.5 * DN_BETA)
    w_in = jnp.concatenate([w_in_pqk, w_in_v], axis=-1)
    pool_w = nrm(ks[5], (L, POOL_GROUPS, POOL_GROUP_DIM, POOL_GROUP_DIM), POOL_GROUP_DIM ** -0.5)
    pool_b = nrm(ks[6], (L, POOL_GROUPS, POOL_GROUP_DIM), 0.02)
    pool_scale = 1.0 + nrm(ks[7], (L, POOL_WIDTH), 0.1)
    w_out = nrm(ks[8], (L, MIX_WIDTH, D), MIX_WIDTH ** -0.5 * DN_BETA)
    ln1_g = 1.0 + nrm(ks[9], (L, D), 0.02)
    ln1_b = nrm(ks[10], (L, D), 0.02)
    peer_wq = nrm(ks[11], (L, D, PEER_HEADS * PEER_KEY_DIM), D ** -0.5)
    peer_sub_keys = nrm(ks[12], (L, 2, PEER_N_KEYS, PEER_HALF_DIM), PEER_HALF_DIM ** -0.5)
    peer_u = nrm(ks[13], (L, PEER_N_EXPERTS, D), D ** -0.5)
    peer_v = nrm(ks[14], (L, PEER_N_EXPERTS, D), DN_BETA)
    ln2_g = 1.0 + nrm(ks[15], (L, D), 0.02)
    ln2_b = nrm(ks[16], (L, D), 0.02)
    return {"x": x, "ln0_g": ln0_g, "ln0_b": ln0_b, "w_in": w_in, "pool_w": pool_w,
            "pool_b": pool_b, "pool_scale": pool_scale, "w_out": w_out, "ln1_g": ln1_g,
            "ln1_b": ln1_b, "peer_wq": peer_wq, "peer_sub_keys": peer_sub_keys,
            "peer_u": peer_u, "peer_v": peer_v, "ln2_g": ln2_g, "ln2_b": ln2_b}

def reference(x, ln0_g, ln0_b, w_in, pool_w, pool_b, pool_scale, w_out, ln1_g, ln1_b,
              peer_wq, peer_sub_keys, peer_u, peer_v, ln2_g, ln2_b):
    h = layer_norm(x, ln0_g, ln0_b)
    for l in range(DEPTH):
        mix = hybrid_mixer(h, w_in[l], pool_w[l], pool_b[l], pool_scale[l], w_out[l])
        h = layer_norm(DN_ALPHA * h + mix, ln1_g[l], ln1_b[l])
        ffn = peer(h, peer_wq[l], peer_sub_keys[l], peer_u[l], peer_v[l])
        h = layer_norm(DN_ALPHA * h + ffn, ln2_g[l], ln2_b[l])
    return h


_drawn_inputs = setup_inputs


def setup_inputs(seed=0):
    import zlib

    import numpy as np

    out = dict(_drawn_inputs(seed))
    spreads = {}
    factors = {}
    for name, (base, spread) in spreads.items():
        noise = np.random.default_rng([zlib.crc32(name.encode()), seed]).standard_normal(out[name].shape)
        drawn = base * np.exp(spread * noise) if base else spread * noise
        out[name] = __import__('jax').numpy.asarray(drawn.astype(out[name].dtype))
    for name, factor in factors.items():
        out[name] = (out[name] * factor).astype(out[name].dtype)
    return out
```

```python
import math
from contextlib import ExitStack

import concourse.bass as bass
from concourse import mybir

F32 = mybir.dt.float32
BF16 = mybir.dt.bfloat16
U32 = mybir.dt.uint32
ALU = mybir.AluOpType
ACT = mybir.ActivationFunctionType
AX = mybir.AxisListType

P = 128
SEQ = 1024
D = 1024
BLOCKS = SEQ // P
DCH = D // P
HALF = 512
POOL_WINDOWS = (2, 4, 8, 16)
GROUPS = len(POOL_WINDOWS)
HEADS = 8
HEAD_DIM = 64
HALVES = 2
PER_HALF = HEADS // HALVES
PEER_HEADS = 8
N_KEYS = 128
TOPK = 16
PICKS = PEER_HEADS * TOPK
UNITS = BLOCKS * PEER_HEADS
LN_EPS = 1e-5
ALPHA = 2.0 ** 0.25
CAP_OPEN = 3.0e38
CAP_SHUT = -1.0e30
LOWEST = -3.0e38
RING = 8
ROW_LEN = [TOPK // (a + 1) for a in range(TOPK)]
ROW_AT = [sum(ROW_LEN[:a]) for a in range(TOPK)]
CANDS = sum(ROW_LEN)


def need(engine, semaphore, value):
    if isinstance(value, int) and value <= 0:
        return
    engine.wait_ge(semaphore, value)


def peeled(engine, count, body):
    body(0)
    with engine.Fori(1, count) as i:
        body(i)


class Steps:

    def __init__(self, engine, semaphore, passed=None):
        self.engine, self.semaphore, self.passed, self.base, self.k = engine, semaphore, passed, 0, 0

    def at(self, base):
        self.base, self.k = base, 0

    def link(self, instruction):
        self.k += 1
        instruction.then_inc(self.semaphore, 1)
        self.engine.wait_ge(self.semaphore, self.base + self.k)
        if self.passed is not None:
            self.engine.sem_inc(self.passed, 1)


def layer_kernel(nc, x, ln0_g, ln0_b, w_in_chunks, w_v, pool_w, pool_b, pool_scale, w_out,
                 ln1_g, ln1_b, wq_chunks, keys_t, peer_u, peer_v, ln2_g, ln2_b, out):
    x_blocks = x.rearrange("(b p) d -> b p d", p=P)
    out_blocks = out.rearrange("(b p) d -> b p d", p=P)
    h0_dram = nc.dram_tensor("h0_scratch", (BLOCKS, P, D), F32).ap()
    x1_dram = nc.dram_tensor("x1_scratch", (BLOCKS, P, D), F32).ap()

    ctx = ExitStack()
    with ctx:
        def sb(name, shape, dt=F32):
            return ctx.enter_context(nc.sbuf_tensor(name, shape, dt))

        def sem(name):
            return ctx.enter_context(nc.semaphore(name))

        KIB = 256
        arena = sb("arena", [P, 196 * KIB])

        def region(kib, cols):
            return arena[:, int(kib * KIB):int(kib * KIB) + cols]

        hT = region(0, DCH * SEQ).rearrange("p (c t) -> p c t", c=DCH)
        u_ring = region(0, RING * D).rearrange("p (s d) -> p s d", s=RING)
        uqk = region(32, 12 * SEQ).rearrange("p (m t) -> p m t", m=12)
        x1_all = region(32, BLOCKS * D).rearrange("p (b d) -> p b d", b=BLOCKS)
        wo = region(80, DCH * D).rearrange("p (c d) -> p c d", c=DCH)
        wv = region(80, DCH * HALF).rearrange("p (c d) -> p c d", c=DCH)
        res = region(80, BLOCKS * D).rearrange("p (b d) -> p b d", b=BLOCKS)
        v_all = region(112, BLOCKS * HALF).rearrange("p (b d) -> p b d", b=BLOCKS)
        w_ring = region(128, 4 * D).rearrange("p (s c n) -> p s c n", s=4, c=DCH)
        v_ring = region(112, RING * D).rearrange("p (s d) -> p s d", s=RING)
        ln_rows = region(144, 2 * D).rearrange("p (r d) -> p r d", r=2)
        xin = region(152, 2 * D).rearrange("p (s d) -> p s d", s=2)
        qpeer = region(152, 2 * D).rearrange("p (s d) -> p s d", s=2)
        normed = region(160, 2 * D).rearrange("p (s d) -> p s d", s=2)
        diag_ring = region(152, RING * P).rearrange("p (s n) -> p s n", s=RING)
        products = region(156, 2 * D).rearrange("p (s d) -> p s d", s=2)
        h0_back = region(152, D)
        x1_pre = region(156, D)
        q_pad = region(168, HEADS * P).rearrange("p (h q) -> p h q", h=HEADS)
        sp = region(172, HEADS * P).rearrange("p (h q) -> p h q", h=HEADS)
        sp_sum = region(176, HEADS * P).rearrange("p (h q) -> p h q", h=HEADS)
        attn = region(180, HEADS * P).rearrange("p (h q) -> p h q", h=HEADS)
        soft = region(184, HEADS * P).rearrange("p (h q) -> p h q", h=HEADS)
        mix_t = region(188, DCH * P).rearrange("p (c q) -> p c q", c=DCH)
        k_stage = region(192, 4 * P).rearrange("p (c k) -> p c k", c=4)
        o_stage = region(194, HALF)
        win_a = region(172, SEQ)
        win_b = region(176, SEQ)
        match = region(168, BLOCKS * TOPK * CANDS).rearrange("p (g c) -> p g c", c=CANDS)
        idx_all = region(64, UNITS * TOPK + TOPK).bitcast(U32)
        gate_all = region(68.25, UNITS * TOPK)
        key_work = region(72.5, BLOCKS * N_KEYS).rearrange("p (b n) -> p b n", b=BLOCKS)

        def small(name, shape, dt=F32):
            return sb(name, shape, dt)

        ident = small("ident", [P, P])
        neg_tri = small("neg_tri", [P, P])
        neg_ones = small("neg_ones", [P, P])
        cap = small("cap", [P, P])
        keys_sb = small("keys_sb", [P, 2, N_KEYS])
        pool_w_sb = small("pool_w_sb", [P, GROUPS, P])
        pool_bs = small("pool_bs", [P, 2, GROUPS])
        kind_scale = small("kind_scale", [P, 3])
        inv_count = small("inv_count", [P, TOPK])
        head_cols = small("head_cols", [P, TOPK])
        iota_c = small("iota_c", [P, CANDS])
        stats = small("stats", [P, 2, 6])
        mean_var = small("mean_var", [P, 2])
        eps_col = small("eps_col", [P, 1])
        one_col = small("one_col", [P, 1])
        lnv = small("lnv", [P, 1])
        rstd0 = small("rstd0", [P, 1])
        newton = small("newton", [P, 1])
        rstd = small("rstd", [P, 1])
        top_s = region(112, 2 * BLOCKS * TOPK).rearrange("p (h b k) -> p h b k", h=2, b=BLOCKS)
        top_i = region(113, 2 * BLOCKS * TOPK).bitcast(U32).rearrange("p (h b k) -> p h b k", h=2, b=BLOCKS)
        top_if = region(114, 2 * BLOCKS * TOPK).rearrange("p (h b k) -> p h b k", h=2, b=BLOCKS)
        cand = region(115, BLOCKS * CANDS).rearrange("p (b k) -> p b k", b=BLOCKS)
        cand_e = region(116.75, BLOCKS * CANDS).rearrange("p (b k) -> p b k", b=BLOCKS)
        cand_w = region(118.5, BLOCKS * CANDS).rearrange("p (b k) -> p b k", b=BLOCKS)
        best_s = region(120.25, BLOCKS * TOPK).rearrange("p (b k) -> p b k", b=BLOCKS)
        best_p = region(120.75, BLOCKS * TOPK).bitcast(U32).rearrange("p (b k) -> p b k", b=BLOCKS)
        best_pf = region(121.25, BLOCKS * TOPK).rearrange("p (b k) -> p b k", b=BLOCKS)
        gate_sum = small("gate_sum", [P, BLOCKS])
        idx_u = small("idx_u", [P, 2, TOPK], U32)
        idx_v = small("idx_v", [P, 2, TOPK], U32)
        hid = small("hid", [P, 2, TOPK])
        hid_g = small("hid_g", [P, 2, TOPK])
        act_g = small("act_g", [P, 2, TOPK])

        bank = ctx.enter_context(nc.psum_tensor("bank", [P, 8, HALF], F32))
        z = bank[:, 0:2, :]
        o_ps = bank[:, 2, :]
        oT_ps = bank[:, 3, :].rearrange("p (c q) -> p c q", c=4)
        y_ps = bank[:, 4:6, :].rearrange("p b n -> p (b n)")
        xT_ps = bank[:, 6:8, :].rearrange("p b (c q) -> p (b c) q", q=P)

        consts = sem("consts_made")
        const_step = sem("const_step")
        ln_loaded = sem("ln_loaded")
        small_loaded = sem("small_weights_loaded")
        x_loaded = [sem(f"x_loaded{i}") for i in range(2)]
        x_free = sem("x_slot_free")
        h0_ready = sem("h0_ready")
        h0_stored = [sem(f"h0_stored{i}") for i in range(2)]
        h0_transposed = sem("h0_transposed")
        h0t_copied = sem("h0t_copied")
        w_loaded = [sem(f"w_loaded{i}") for i in range(4)]
        wv_loaded = sem("wv_loaded")
        wo_loaded = sem("wo_loaded")
        proj_done = sem("proj_done")
        proj_copied = sem("proj_copied")
        v_done = sem("v_done")
        v_copied = sem("v_copied")
        pooled = sem("pooled")
        pool_mm = sem("pool_mm_done")
        pool_mixed = sem("pool_mixed")
        var_ready = sem("var_ready")
        rstd0_ready = sem("rstd0_ready")
        act_step = sem("act_step")
        pool_passed = sem("pool_passed_wait")
        dve_passed = sem("dve_passed_wait")
        dve_a = sem("dve_step_a")
        dve_b = sem("dve_step_b")
        dve_c = sem("dve_step_c")
        dve_d = sem("dve_step_d")
        dve_e = sem("dve_step_e")
        q_staged = sem("q_staged")
        k_staged = sem("k_staged")
        z_done = sem("z_done")
        z_capped = sem("z_capped")
        ln_ready = sem("ln_ready")
        sp_ready = sem("sp_ready")
        sum_zeroed = sem("sum_zeroed")
        sum_ready = sem("sum_ready")
        c_done = sem("c_done")
        a_ready = sem("a_ready")
        av_done = sem("av_done")
        o_copied = sem("o_copied")
        o_transposed = sem("o_transposed")
        mix_copied = sem("mix_copied")
        mixp_staged = sem("mixp_staged")
        y_done = sem("y_done")
        y_read = sem("y_read")
        h0_reloaded = sem("h0_reloaded")
        x1_ready = sem("x1_ready")
        x1_transposed = sem("x1_transposed")
        x1t_copied = sem("x1t_copied")
        x1_stored = sem("x1_stored")
        wq_done = sem("wq_done")
        qp_copied = sem("qp_copied")
        score_ready = sem("score_ready")
        score_free = sem("score_bank_free")
        gate_in = sem("gate_in_ready")
        gate_exp = sem("gate_exp_ready")
        x1_back = sem("x1_back")
        res_init = sem("residual_scaled")
        idx_u_staged = sem("idx_u_staged")
        idx_v_staged = sem("idx_v_staged")
        u_loaded = [sem(f"u_loaded{i}") for i in range(RING)]
        v_loaded = [sem(f"v_loaded{i}") for i in range(RING)]
        u_free = sem("u_slot_free")
        pick_free = sem("pick_slot_free")
        gelu_done = sem("gelu_done")
        act_ready = sem("act_ready")
        diag_ready = sem("diag_ready")
        f_free = sem("f_bank_free")
        out_ready = sem("out_ready")
        out_stored = [sem(f"out_stored{i}") for i in range(2)]

        block = ctx.enter_context(nc.Block())

        def block_of(ap, n):
            return ap[bass.ds(n, 1)].rearrange("o p d -> p (o d)")

        def cols(n, width=P):
            return bass.ds(n * width, width)

        def pairs_before(b):
            return b * (b + 1) // 2

        def first_step(engine, b):
            return engine.snap(engine.snap((b - 1) * (b + 2) // 2) + 1)

        def later_before(b):
            return b * (b - 1) // 2

        def key_block(b, i):
            if isinstance(b, int):
                return b - i
            return nc.s_assert_within(b - i, 0, BLOCKS - 1, skip_runtime_bounds_check_because="i runs from 0 to b")

        @block.sync
        def _(sync):
            def load_ln(g, b):
                sync.dma_start(ln_rows[:, 0, :], g.partition_broadcast(P)).then_inc(ln_loaded, 16)
                sync.dma_start(ln_rows[:, 1, :], b.partition_broadcast(P)).then_inc(ln_loaded, 16)

            load_ln(ln0_g, ln0_b)
            with sync.Fori(0, BLOCKS // 2) as i:
                for par in range(2):
                    n = 2 * i + par
                    sync.wait_ge(x_free, n + 1)
                    sync.dma_start(xin[:, par, :], block_of(x_blocks, n)).then_inc(x_loaded[par], 16)
            with sync.Fori(1, 3) as kind:
                for s in range(4):
                    sync.wait_ge(proj_done, 4 * kind + s - 3)
                    sync.dma_start(w_ring[:, s], w_in_chunks[bass.ds(4 * kind + s, 1)].rearrange("o p c n -> p (o c) n")).then_inc(w_loaded[s], 16)
            sync.wait_ge(h0_ready, BLOCKS)
            load_ln(ln1_g, ln1_b)
            for s in range(4):
                sync.wait_ge(proj_done, 9 + s)
                sync.dma_start(w_ring[:, s], wq_chunks[s]).then_inc(w_loaded[s], 16)
            sync.wait_ge(v_done, BLOCKS)
            sync.dma_start(wo, w_out.rearrange("(c p) d -> p c d", p=P)).then_inc(wo_loaded, 16)
            for par in range(2):
                sync.wait_ge(h0_stored[par], 16 * (BLOCKS // 2))
            def stage_c_block(b):
                need(sync, y_read, b)
                sync.dma_start(h0_back, block_of(h0_dram, b)).then_inc(h0_reloaded, 16)
                sync.wait_ge(x1_ready, b + 1)
                sync.dma_start(block_of(x1_dram, b), normed[:, 0, :]).then_inc(x1_stored, 16)

            peeled(sync, BLOCKS, stage_c_block)
            load_ln(ln2_g, ln2_b)
            sync.wait_ge(x1_stored, 16 * BLOCKS)
            sync.wait_ge(wq_done, 1)
            sync.dma_start(x1_all, x1_dram.rearrange("b p d -> p b d")).then_inc(x1_back, 16)
            with sync.Fori(1, 4) as i:
                for s in range(4):
                    sync.wait_ge(wq_done, 4 * i + s - 3)
                    sync.dma_start(w_ring[:, s], wq_chunks[bass.ds(4 * i + s, 1)].rearrange("o p c n -> p (o c) n")).then_inc(w_loaded[s], 16)
            with sync.Fori(0, BLOCKS // 2) as i:
                for par in range(2):
                    n = 2 * i + par
                    sync.wait_ge(out_ready, n + 1)
                    sync.dma_start(block_of(out_blocks, n), normed[:, par, :]).then_inc(out_stored[par], 16)
            for par in range(2):
                sync.wait_ge(out_stored[par], 16 * (BLOCKS // 2))

        @block.gpsimd
        def _(pool):
            pool.memset(ident[:], 0.0)
            pool.memset(neg_tri[:], -1.0)
            pool.memset(neg_ones[:], -1.0)
            pool.memset(cap[:], CAP_OPEN)
            pool.memset(kind_scale[:], 1.0)
            pool.memset(eps_col[:], LN_EPS)
            pool.memset(one_col[:], 1.0)
            pool.memset(q_pad, 0.0)
            pool.memset(idx_u[:], 0)
            pool.iota(iota_c[:], pattern=[[1, CANDS]], base=0, channel_multiplier=0, allow_small_or_imprecise_dtypes=True)
            pool.iota(inv_count[:], pattern=[[1, TOPK]], base=1, channel_multiplier=0, allow_small_or_imprecise_dtypes=True).then_inc(const_step, 1)
            pool.wait_ge(const_step, 1)
            pool.affine_select(out=ident[:], in_=ident[:], compare_op=ALU.not_equal, fill=1.0, base=0,
                               pattern=[[-1, P]], channel_multiplier=1)
            pool.affine_select(out=neg_tri[:], in_=neg_tri[:], compare_op=ALU.is_ge, fill=0.0, base=0,
                               pattern=[[-1, P]], channel_multiplier=1)
            pool.affine_select(out=cap[:], in_=cap[:], compare_op=ALU.is_gt, fill=CAP_SHUT, base=0,
                               pattern=[[1, P]], channel_multiplier=-1)
            pool.memset(kind_scale[:, 1:2], HEAD_DIM ** -0.5).then_inc(consts, 1)
            with pool.Fori(0, BLOCKS // 2) as i:
                for par in range(2):
                    n = 2 * i + par
                    pool.wait_ge(h0_ready, n + 1)
                    pool.dma_start(block_of(h0_dram, n), normed[:, par, :]).then_inc(h0_stored[par], 16)

            def begin_block(b, n):
                need(pool, z_done, 2 * n)
                pool.tensor_copy(k_stage, uqk[:, 8:12, cols(b)]).then_inc(k_staged, 1)
                need(pool, c_done, 2 * n)
                pool.sem_inc(pool_passed, 1)
                pool.memset(sp_sum, 0.0).then_inc(sum_zeroed, 1)
                pool.wait_ge(sum_zeroed, b + 1)
                need(pool, y_done, b)
                pool.tensor_copy(mix_t[:, 0:4, :], uqk[:, 0:4, cols(b)]).then_inc(mixp_staged, 1)

            def later_keys(b, i, n):
                pool.wait_ge(z_done, 2 * n)
                pool.tensor_copy(k_stage, uqk[:, 8:12, cols(key_block(b, i))]).then_inc(k_staged, 1)
                for c in range(HALVES):
                    hs = slice(c * PER_HALF, (c + 1) * PER_HALF)
                    pool.wait_ge(sp_ready, 2 * n + c - 1)
                    pool.wait_ge(c_done, 2 * n + c - 1)
                    pool.tensor_tensor(sp_sum[:, hs], sp_sum[:, hs], sp[:, hs], ALU.add).then_inc(sum_ready, 1)

            pool.wait_ge(proj_copied, 12)
            pool.wait_ge(pool_mixed, GROUPS)
            begin_block(0, 0)
            with pool.Fori(1, BLOCKS) as b:
                first = first_step(pool, b)
                begin_block(b, first)
                with pool.Fori(1, b + 1) as i:
                    later_keys(b, i, pool.snap(first + i))

            pool.wait_ge(x1_back, 16)
            pool.wait_ge(y_done, BLOCKS)
            for b in range(BLOCKS):
                pool.tensor_scalar(res[:, b, :], x1_all[:, b, :], ALPHA, 0.0, ALU.mult, ALU.add).then_inc(res_init, 1)

            def gathers(u_unit, u_par, v_unit, v_par):
                if u_unit is not None:
                    pool.wait_ge(idx_u_staged, u_unit + 1)
                if v_unit is not None:
                    pool.wait_ge(idx_v_staged, v_unit + 1)
                for k in range(TOPK):
                    s = k % RING
                    if u_unit is not None:
                        pool.wait_ge(u_free, TOPK * u_unit + k + 1)
                        pool.sem_inc(pool_passed, 1)
                        pool.indirect_dma_start(u_ring[:, s, :], None, peer_u,
                                                bass.IndirectOffsetOnAxis(ap=idx_u[:, u_par, k:k + 1], axis=0)).then_inc(u_loaded[s], 16)
                    if v_unit is not None:
                        pool.wait_ge(pick_free, TOPK * v_unit + k + 1)
                        pool.sem_inc(pool_passed, 1)
                        pool.indirect_dma_start(v_ring[:, s, :], None, peer_v,
                                                bass.IndirectOffsetOnAxis(ap=idx_v[:, v_par, k:k + 1], axis=0)).then_inc(v_loaded[s], 16)

            gathers(0, 0, None, 0)
            gathers(1, 1, 0, 0)
            with pool.Fori(1, UNITS // 2) as i:
                gathers(2 * i, 0, 2 * i - 1, 1)
                gathers(2 * i + 1, 1, 2 * i, 0)
            gathers(None, 0, UNITS - 1, 1)

        @block.scalar
        def _(act):
            def rsqrt_seed(n):
                act.wait_ge(var_ready, n + 1)
                act.activation(lnv[:], mean_var[:, 1:2], ACT.Ln, bias=eps_col[:]).then_inc(act_step, 1)
                act.wait_ge(act_step, n + 1)
                act.activation(rstd0[:], lnv[:], ACT.Exp, scale=-0.5).then_inc(rstd0_ready, 1)

            act.preload_act_table_set("natural_log_exp_and_others")
            for s in range(4):
                act.dma_start(w_ring[:, s], w_in_chunks[s]).then_inc(w_loaded[s], 16)
            act.dma_start(pool_w_sb[:], pool_w.rearrange("g c d -> c g d")).then_inc(small_loaded, 16)
            act.dma_start(pool_bs[:, 0, :], pool_b).then_inc(small_loaded, 16)
            act.dma_start(pool_bs[:, 1, :], pool_scale).then_inc(small_loaded, 16)
            act.dma_start(keys_sb[:], keys_t.rearrange("h c n -> c h n")).then_inc(small_loaded, 16)
            act.dma_start(wv, w_v.rearrange("(c p) n -> p c n", p=P)).then_inc(wv_loaded, 16)
            act.wait_ge(consts, 1)
            with act.Fori(0, BLOCKS // 2) as i:
                for par in range(2):
                    n = 2 * i + par
                    rsqrt_seed(n)
                    act.wait_ge(h0_transposed, n + 1)
                    act.activation(hT[:, :, cols(n)], bank[:, 2 * par:2 * par + 2, :].rearrange("p b (c q) -> p (b c) q", q=P),
                                   ACT.Copy).then_inc(h0t_copied, 1)
            with act.Fori(0, 3) as kind:
                for s in range(4):
                    act.wait_ge(proj_done, 4 * kind + s + 1)
                    act.activation(uqk[:, bass.ds(4 * kind + s, 1), :].rearrange("p o t -> p (o t)"),
                                   bank[:, 2 * s:2 * s + 2, :].rearrange("p b n -> p (b n)"), ACT.Copy,
                                   scale=kind_scale[:, bass.ds(kind, 1)]).then_inc(proj_copied, 1)
            for b in range(BLOCKS):
                act.wait_ge(v_done, b + 1)
                act.activation(v_all[:, b, :], bank[:, b, :], ACT.Copy).then_inc(v_copied, 1)

            def stage_queries(b, n):
                need(act, z_done, 2 * n)
                act.activation(q_pad[0:64, 0:HEADS:2, :], uqk[0:64, 4:8, cols(b)], ACT.Copy)
                act.activation(q_pad[64:128, 1:HEADS:2, :], uqk[64:128, 4:8, cols(b)], ACT.Copy).then_inc(q_staged, 1)

            def softplus_and_weights(n, steps_at, diagonal_of=None):
                for c in range(HALVES):
                    hs = slice(c * PER_HALF, (c + 1) * PER_HALF)
                    if diagonal_of is None:
                        act.wait_ge(z_done, 2 * n + c + 1)
                    else:
                        act.wait_ge(z_capped, 2 * diagonal_of + c + 1)
                    need(act, sp_ready, 2 * n + c - 1)
                    act.activation(soft[:, hs], z[:, c, :].rearrange("p (h q) -> p h q", q=P), ACT.Abs).then_inc(act_step, 1)
                    act.wait_ge(act_step, steps_at + 2 * c + 1)
                    act.activation(soft[:, hs], soft[:, hs], ACT.Exp, scale=-1.0).then_inc(act_step, 1)
                    act.wait_ge(act_step, steps_at + 2 * c + 2)
                    act.activation(soft[:, hs], soft[:, hs], ACT.Ln, bias=one_col[:]).then_inc(ln_ready, 1)
                for c in range(HALVES):
                    hs = slice(c * PER_HALF, (c + 1) * PER_HALF)
                    act.wait_ge(c_done, 2 * n + c + 1)
                    need(act, av_done, 2 * n + c - 1)
                    act.activation(attn[:, hs], z[:, c, :].rearrange("p (h q) -> p h q", q=P), ACT.Exp).then_inc(a_ready, 1)

            def finish_attention(b, n_end):
                act.wait_ge(av_done, 2 * n_end)
                act.activation(o_stage, o_ps, ACT.Copy).then_inc(o_copied, 1)
                act.wait_ge(o_transposed, b + 1)
                need(act, y_done, b)
                act.activation(mix_t[:, 4:8, :], oT_ps, ACT.Copy).then_inc(mix_copied, 1)

            def x1_transpose_out(b):
                act.wait_ge(x1_transposed, b + 1)
                act.activation(hT[:, :, cols(b)], xT_ps, ACT.Copy).then_inc(x1t_copied, 1)

            stage_queries(0, 0)
            softplus_and_weights(0, BLOCKS, 0)
            finish_attention(0, 1)
            with act.Fori(1, BLOCKS) as b:
                first = first_step(act, b)
                stage_queries(b, first)
                softplus_and_weights(first, 4 * first + BLOCKS + b - 1, b)
                act.wait_ge(var_ready, BLOCKS + b)
                act.activation(lnv[:], mean_var[:, 1:2], ACT.Ln, bias=eps_col[:]).then_inc(act_step, 1)
                act.wait_ge(act_step, 4 * first + BLOCKS + b + 4)
                act.activation(rstd0[:], lnv[:], ACT.Exp, scale=-0.5).then_inc(rstd0_ready, 1)
                x1_transpose_out(b - 1)
                with act.Fori(1, b + 1) as i:
                    n = act.snap(first + i)
                    softplus_and_weights(n, 4 * n + BLOCKS + b)
                finish_attention(b, first + b + 1)
            total = 4 * pairs_before(BLOCKS) + BLOCKS + BLOCKS - 1
            act.wait_ge(var_ready, 2 * BLOCKS)
            act.activation(lnv[:], mean_var[:, 1:2], ACT.Ln, bias=eps_col[:]).then_inc(act_step, 1)
            act.wait_ge(act_step, total + 1)
            act.activation(rstd0[:], lnv[:], ACT.Exp, scale=-0.5).then_inc(rstd0_ready, 1)
            x1_transpose_out(BLOCKS - 1)
            def gate_exps(h):
                act.wait_ge(gate_in, h + 1)
                act.activation(best_s, best_s, ACT.Exp).then_inc(gate_exp, 1)

            def query_copies(i):
                for s in range(4):
                    act.wait_ge(wq_done, 4 * i + s + 1)
                    act.activation(qpeer[:, s % 2, :], bank[:, 2 * (s % 2):2 * (s % 2) + 2, :].rearrange("p b n -> p (b n)"),
                                   ACT.Copy).then_inc(qp_copied, 1)
                    if s % 2 and not (isinstance(i, int) and s == 1):
                        gate_exps(2 * i + s // 2 - 1)

            peeled(act, 4, query_copies)
            gate_exps(PEER_HEADS - 1)

            with act.Fori(0, UNITS // 2) as i:
                for par in range(2):
                    n = 2 * i + par
                    act.wait_ge(u_free, RING + TOPK * (n + 1))
                    act.activation(hid_g[:, par, :], hid[:, par, :], ACT.Gelu).then_inc(gelu_done, 1)
                    act.wait_ge(act_ready, n + 1)
                    for k in range(TOPK):
                        act.wait_ge(pick_free, TOPK * n + k + 1)
                        act.activation(diag_ring[:, k % RING, :], ident[:], ACT.Copy, scale=act_g[:, par, k:k + 1]).then_inc(diag_ready, 1)
            act.preload_act_table_set("natural_log_exp_and_others")
            with act.Fori(0, BLOCKS) as b:
                act.wait_ge(var_ready, 2 * BLOCKS + b + 1)
                act.activation(lnv[:], mean_var[:, 1:2], ACT.Ln, bias=eps_col[:]).then_inc(act_step, 1)
                act.wait_ge(act_step, total + 2 + b)
                act.activation(rstd0[:], lnv[:], ACT.Exp, scale=-0.5).then_inc(rstd0_ready, 1)

        @block.tensor
        def _(pe):
            pe.wait_ge(consts, 1)
            def transpose_pair(i):
                for par in range(2):
                    pe.wait_ge(h0_ready, 2 * i + par + 1)
                    need(pe, h0t_copied, 2 * i)
                    for c in range(DCH):
                        mm = pe.transpose(bank[:, 2 * par + c // 4, cols(c % 4)], normed[:, par, cols(c)], ident[:])
                    mm.then_inc(h0_transposed, 1)

            peeled(pe, BLOCKS // 2, transpose_pair)
            pe.wait_ge(h0t_copied, BLOCKS)
            def project_chunks(kind):
                need(pe, proj_copied, 4 * kind)
                for s in range(4):
                    pe.wait_ge(w_loaded[s], 16 * (kind + 1))
                    for half in range(2):
                        for c in range(DCH):
                            mm = pe.matmul(bank[:, 2 * s + half, :], w_ring[:, s, c, :], hT[:, c, cols(half, HALF)],
                                           start=(c == 0), stop=(c == DCH - 1))
                    mm.then_inc(proj_done, 1)

            peeled(pe, 3, project_chunks)
            pe.wait_ge(wv_loaded, 16)
            pe.wait_ge(proj_copied, 12)
            for b in range(BLOCKS):
                for c in range(DCH):
                    mm = pe.matmul(bank[:, b, :], hT[:, c, cols(b)], wv[:, c, :], start=(c == 0), stop=(c == DCH - 1))
                mm.then_inc(v_done, 1)
            pe.wait_ge(small_loaded, 64)
            for g in range(GROUPS):
                pe.wait_ge(v_copied, 2 * g + 2)
                pe.wait_ge(pooled, g + 1)
                for half in range(2):
                    mm = pe.matmul(bank[:, 2 * g + half, :], pool_w_sb[:, g, :], uqk[:, g, cols(half, HALF)], start=True, stop=True)
                mm.then_inc(pool_mm, 1)
            pe.wait_ge(pool_mixed, GROUPS)

            def attention_step(b, i, n, m=0):
                diagonal = isinstance(i, int) and i == 0
                pe.wait_ge(k_staged, n + 1)
                if diagonal:
                    pe.wait_ge(q_staged, b + 1)
                for c in range(HALVES):
                    need(pe, a_ready, 2 * n + c - 1)
                    for hh in range(PER_HALF):
                        h = c * PER_HALF + hh
                        mm = pe.matmul(z[:, c, cols(hh)], k_stage[:, h // 2, :], q_pad[:, h, :], start=(hh == 0), stop=True, skip_group_check=True)
                    mm.then_inc(z_done, 1)
                for c in range(HALVES):
                    hs = slice(c * PER_HALF, (c + 1) * PER_HALF)
                    pe.wait_ge(sp_ready, 2 * n + c + 1)
                    mm = pe.matmul(z[:, c, :], neg_tri[:], sp[:, hs].rearrange("p h q -> p (h q)"), start=False, stop=True, skip_group_check=True)
                    if not diagonal:
                        pe.wait_ge(sum_ready, 2 * m + c + 1)
                        mm = pe.matmul(z[:, c, :], neg_ones[:], sp_sum[:, hs].rearrange("p h q -> p (h q)"), start=False, stop=True, skip_group_check=True)
                    mm.then_inc(c_done, 1)
                if diagonal:
                    need(pe, o_copied, b)
                for c in range(HALVES):
                    pe.wait_ge(a_ready, 2 * n + c + 1)
                    for hh in range(PER_HALF):
                        h = c * PER_HALF + hh
                        mm = pe.matmul(o_ps[:, cols(h, HEAD_DIM)], attn[:, h, :],
                                       v_all[:, bass.ds(key_block(b, i), 1), cols(h, HEAD_DIM)].rearrange("p o d -> p (o d)"),
                                       start=(diagonal and h == 0), stop=True, skip_group_check=True)
                    mm.then_inc(av_done, 1)

            def output_projection(b):
                pe.wait_ge(o_copied, b + 1)
                for c in range(4):
                    mm = pe.transpose(oT_ps[:, c, :], o_stage[:, cols(c)], ident[:])
                mm.then_inc(o_transposed, 1)
                pe.wait_ge(mixp_staged, b + 1)
                pe.wait_ge(mix_copied, b + 1)
                need(pe, y_read, b)
                for half in range(2):
                    for c in range(DCH):
                        mm = pe.matmul(y_ps[:, cols(half, HALF)], mix_t[:, c, :], wo[:, c, cols(half, HALF)], start=(c == 0), stop=(c == DCH - 1))
                mm.then_inc(y_done, 1)

            def x1_transposes(b):
                pe.wait_ge(x1_ready, b + 1)
                need(pe, x1t_copied, b)
                for c in range(DCH):
                    mm = pe.transpose(xT_ps[:, c, :], normed[:, 0, cols(c)], ident[:])
                mm.then_inc(x1_transposed, 1)

            pe.wait_ge(wo_loaded, 16)
            attention_step(0, 0, 0)
            output_projection(0)
            with pe.Fori(1, BLOCKS) as b:
                first = first_step(pe, b)
                attention_step(b, 0, first)
                x1_transposes(b - 1)
                with pe.Fori(1, b + 1) as i:
                    attention_step(b, i, pe.snap(first + i), pe.snap(later_before(b) + (i - 1)))
                output_projection(b)
            x1_transposes(BLOCKS - 1)
            pe.wait_ge(x1t_copied, BLOCKS)
            def query_chunks(i):
                for s in range(4):
                    par = s % 2
                    pe.wait_ge(w_loaded[s], 16 * (i + 4))
                    need(pe, qp_copied, 4 * i + s)
                    for half in range(2):
                        for c in range(DCH):
                            mm = pe.matmul(bank[:, 2 * par + half, :], w_ring[:, s, c, :], hT[:, c, cols(half, HALF)],
                                           start=(c == 0), stop=(c == DCH - 1))
                    mm.then_inc(wq_done, 1)
                    pe.wait_ge(qp_copied, 4 * i + s + 1)
                    pe.wait_ge(score_free, 4 * i + s + 1)
                    for b in range(BLOCKS):
                        mm = pe.matmul(bank[:, 4 + 2 * par + b // 4, cols(b % 4)], qpeer[:, par, cols(b)], keys_sb[:, s % 2, :], start=True, stop=True)
                    mm.then_inc(score_ready, 1)

            peeled(pe, 4, query_chunks)
            pe.sem_inc(pick_free, RING)
            with pe.Fori(0, UNITS // 2) as i:
                for par in range(2):
                    n = 2 * i + par
                    pe.wait_ge(f_free, n + 1)
                    for k in range(TOPK):
                        s = k % RING
                        pe.wait_ge(diag_ready, TOPK * n + k + 1)
                        pe.wait_ge(v_loaded[s], 16 * (2 * n + k // RING + 1))
                        for half in range(2):
                            mm = pe.matmul(bank[:, 4 * par + half, :], diag_ring[:, s, :], v_ring[:, s, cols(half, HALF)],
                                           start=(k == 0), stop=(k == TOPK - 1))
                        mm.then_inc(pick_free, 1)

        @block.vector
        def _(dve):
            def layer_norm(steps, n, src, dst, before_write, release=None):
                dve.bn_stats(stats[:, 0, :], src[:, 0:HALF])
                steps.link(dve.bn_stats(stats[:, 1, :], src[:, HALF:D]))
                dve.bn_aggr(mean_var[:], stats[:]).then_inc(var_ready, 1)
                dve.wait_ge(var_ready, n + 1)
                before_write()
                m = dve.scalar_tensor_tensor(dst, src, mean_var[:, 0:1], ln_rows[:, 0, :], ALU.subtract, ALU.mult)
                if release is not None:
                    m.then_inc(release, 1)
                dve.wait_ge(rstd0_ready, n + 1)
                steps.link(dve.tensor_tensor(newton[:], rstd0[:], rstd0[:], ALU.mult))
                steps.link(dve.scalar_tensor_tensor(newton[:], mean_var[:, 1:2], LN_EPS, newton[:], ALU.add, ALU.mult))
                steps.link(dve.tensor_scalar(newton[:], newton[:], -0.5, 1.5, ALU.mult, ALU.add))
                steps.link(dve.tensor_tensor(rstd[:], rstd0[:], newton[:], ALU.mult))
                return dve.scalar_tensor_tensor(dst, dst, rstd[:], ln_rows[:, 1, :], ALU.mult, ALU.add)

            LN_LINKS = 5
            dve.sem_inc(x_free, 2)
            dve.wait_ge(consts, 1)
            steps = Steps(dve, dve_a, dve_passed)
            steps.link(dve.reciprocal(inv_count[:], inv_count[:]))
            dve.wait_ge(ln_loaded, 32)
            def norm_pair(i):
                steps.at(2 * LN_LINKS * i + 1)
                for par in range(2):
                    n = 2 * i + par
                    dve.wait_ge(x_loaded[par], 16 * (i + 1))

                    def slot_free():
                        need(dve, h0_transposed, 2 * i)
                        need(dve, h0_stored[par], 16 * i)

                    layer_norm(steps, n, xin[:, par, :], normed[:, par, :], slot_free, x_free).then_inc(h0_ready, 1)
                assert steps.k == 2 * LN_LINKS

            peeled(dve, BLOCKS // 2, norm_pair)
            steps = Steps(dve, dve_b)
            dve.wait_ge(small_loaded, 64)
            for g, w in enumerate(POOL_WINDOWS):
                dve.wait_ge(proj_copied, g + 1)
                u = uqk[:, g, :]
                cur, step = u, 1
                spare = [win_a, win_b]
                while step < w:
                    dst = spare.pop(0)
                    dve.tensor_tensor(dst[:, step:], cur[:, step:], cur[:, :SEQ - step], ALU.add)
                    steps.link(dve.tensor_copy(dst[:, :step], cur[:, :step]))
                    if cur is not u:
                        spare.append(cur)
                    cur, step = dst, 2 * step
                steps.link(dve.tensor_tensor(head_cols[:, :w - 1], cur[:, :w - 1], inv_count[:, :w - 1], ALU.mult))
                steps.link(dve.tensor_tensor(head_cols[:, :w - 1], head_cols[:, :w - 1], u[:, :w - 1], ALU.subtract))
                steps.link(dve.scalar_tensor_tensor(u, cur, 1.0 / w, u, ALU.mult, ALU.subtract))
                dve.tensor_copy(u[:, :w - 1], head_cols[:, :w - 1]).then_inc(pooled, 1)
            for g in range(GROUPS):
                dve.wait_ge(pool_mm, g + 1)
                dve.tensor_scalar(uqk[:, g, :], bank[:, 2 * g:2 * g + 2, :].rearrange("p b n -> p (b n)"),
                                  pool_bs[:, 0, g:g + 1], pool_bs[:, 1, g:g + 1], ALU.add, ALU.mult).then_inc(pool_mixed, 1)

            steps = Steps(dve, dve_c, dve_passed)

            def softplus(b, i, n, m=0):
                diagonal = isinstance(i, int) and i == 0
                if diagonal:
                    for c in range(HALVES):
                        zc = z[:, c, :].rearrange("p (h q) -> p h q", q=P)
                        dve.wait_ge(z_done, 2 * n + c + 1)
                        dve.tensor_tensor(zc, zc, cap[:].unsqueeze(1).broadcast_to([P, PER_HALF, P]), ALU.min).then_inc(z_capped, 1)
                for c in range(HALVES):
                    hs = slice(c * PER_HALF, (c + 1) * PER_HALF)
                    zc = z[:, c, :].rearrange("p (h q) -> p h q", q=P)
                    dve.wait_ge(ln_ready, 2 * n + c + 1)
                    need(dve, c_done, 2 * n + c - 1)
                    if not diagonal:
                        dve.wait_ge(sum_ready, 2 * m + c + 1)
                    dve.scalar_tensor_tensor(sp[:, hs], zc, 0.0, soft[:, hs], ALU.max, ALU.add).then_inc(sp_ready, 1)

            def norm_1(b):
                dve.wait_ge(h0_reloaded, 16 * (b + 1))
                dve.wait_ge(y_done, b + 1)
                dve.scalar_tensor_tensor(x1_pre, h0_back, ALPHA, y_ps, ALU.mult, ALU.add).then_inc(y_read, 1)
                dve.wait_ge(y_read, b + 1)

                def slot_free():
                    need(dve, x1_transposed, b)
                    need(dve, x1_stored, 16 * b)

                layer_norm(steps, BLOCKS + b, x1_pre, normed[:, 0, :], slot_free).then_inc(x1_ready, 1)

            softplus(0, 0, 0)
            dve.wait_ge(ln_loaded, 64)
            dve.wait_ge(h0_transposed, BLOCKS)
            dve.wait_ge(h0_stored[0], 16 * (BLOCKS // 2))
            dve.wait_ge(h0_stored[1], 16 * (BLOCKS // 2))
            c_links = LN_LINKS
            with dve.Fori(1, BLOCKS) as b:
                steps.at(c_links * b - LN_LINKS)
                first = first_step(dve, b)
                softplus(b, 0, first)
                norm_1(b - 1)
                assert steps.k == c_links
                with dve.Fori(1, b + 1) as i:
                    softplus(b, i, dve.snap(first + i), dve.snap(later_before(b) + (i - 1)))
            steps.at(c_links * BLOCKS - LN_LINKS)
            norm_1(BLOCKS - 1)

            steps = Steps(dve, dve_d, dve_passed)
            dve.sem_inc(score_free, 2)

            def top16(values, work, out_s, out_i, release=None):
                n = len(values)
                for j in range(n):
                    m = dve.max(out_s(j)[:, 0:8], values[j])
                steps.link(m)
                for j in range(n):
                    m = dve.max_index(out_i(j)[:, 0:8], out_s(j)[:, 0:8], values[j])
                for j in range(n):
                    m = dve.match_replace(work(j), out_s(j)[:, 0:8], values[j], LOWEST)
                steps.link(m)
                for j in range(n):
                    m = dve.max(out_s(j)[:, 8:16], work(j))
                steps.link(m)
                for j in range(n):
                    m = dve.max_index(out_i(j)[:, 8:16], out_s(j)[:, 8:16], work(j))
                steps.link(m)

            d_links = 2 * (2 * 4 + 4 + 10)
            with dve.Fori(0, 4) as i:
                steps.at(d_links * i)
                for s in range(4):
                    half = s % 2
                    dve.wait_ge(score_ready, 4 * i + s + 1)
                    dve.sem_inc(dve_passed, 1)
                    score = [bank[:, 4 + 2 * half + b // 4, cols(b % 4)] for b in range(BLOCKS)]
                    top16(score, lambda b: key_work[:, b, :], lambda b: top_s[:, half, b, :], lambda b: top_i[:, half, b, :])
                    dve.tensor_copy(top_if[:, half], top_i[:, half]).then_inc(score_free, 1)
                    if not half:
                        continue
                    h = 2 * i + s // 2
                    dve.wait_ge(score_free, 4 * i + s + 3)
                    steps.link(dve.tensor_scalar(top_if[:, 0], top_if[:, 0], float(N_KEYS), None, ALU.mult))
                    for lists, dst in ((top_s, cand), (top_if, cand_e)):
                        for a in range(5):
                            n = ROW_LEN[a]
                            m = dve.tensor_tensor(dst[:, :, ROW_AT[a]:ROW_AT[a] + n], lists[:, 1, :, 0:n],
                                                  lists[:, 0, :, a:a + 1].broadcast_to([P, BLOCKS, n]), ALU.add)
                        m = dve.tensor_tensor(dst[:, :, ROW_AT[5]:ROW_AT[8]].rearrange("p b (a n) -> p b a n", n=2),
                                              lists[:, 1, :, 0:2].unsqueeze(2).broadcast_to([P, BLOCKS, 3, 2]),
                                              lists[:, 0, :, 5:8].unsqueeze(3).broadcast_to([P, BLOCKS, 3, 2]), ALU.add)
                        m = dve.tensor_tensor(dst[:, :, ROW_AT[8]:CANDS], lists[:, 0, :, 8:16],
                                              lists[:, 1, :, 0:1].broadcast_to([P, BLOCKS, 8]), ALU.add)
                    steps.link(m)
                    top16([cand[:, b, :] for b in range(BLOCKS)], lambda b: cand_w[:, b, :],
                          lambda b: best_s[:, b, :], lambda b: best_p[:, b, :])
                    steps.link(dve.tensor_copy(best_pf, best_p))
                    flat_p = best_pf.rearrange("p b k -> p (b k)")
                    steps.link(dve.tensor_tensor(match, iota_c[:].unsqueeze(1).broadcast_to([P, BLOCKS * TOPK, CANDS]),
                                                 flat_p.unsqueeze(2).broadcast_to([P, BLOCKS * TOPK, CANDS]), ALU.is_equal))
                    match4 = match.rearrange("p (b k) c -> p b k c", k=TOPK)
                    steps.link(dve.tensor_tensor(match4, match4, cand_e.unsqueeze(2).broadcast_to([P, BLOCKS, TOPK, CANDS]), ALU.mult))
                    steps.link(dve.tensor_reduce(flat_p, match, AX.X, ALU.add))
                    idx_h = idx_all[:, 0:UNITS * TOPK].rearrange("p (b m) -> p b m", b=BLOCKS)[:, :, cols(h, TOPK)]
                    gate_h = gate_all.rearrange("p (b m) -> p b m", b=BLOCKS)[:, :, cols(h, TOPK)]
                    dve.tensor_copy(idx_h, best_pf)
                    steps.link(dve.tensor_copy(gate_sum[:], best_s[:, :, 0]))
                    dve.tensor_tensor(best_s, best_s, gate_sum[:].unsqueeze(2).broadcast_to([P, BLOCKS, TOPK]), ALU.subtract).then_inc(gate_in, 1)
                    dve.wait_ge(gate_exp, h + 1)
                    steps.link(dve.tensor_reduce(gate_sum[:], best_s, AX.X, ALU.add))
                    steps.link(dve.reciprocal(gate_sum[:], gate_sum[:]))
                    steps.link(dve.tensor_tensor(gate_h, best_s, gate_sum[:].unsqueeze(2).broadcast_to([P, BLOCKS, TOPK]), ALU.mult))
                assert steps.k == d_links, steps.k
            steps.at(4 * d_links)
            steps.link(dve.memset(idx_all[:, UNITS * TOPK:], 0))
            dve.sem_inc(u_free, RING)
            dve.sem_inc(f_free, 2)
            dve.wait_ge(res_init, BLOCKS)
            dve.wait_ge(x1_back, 16)
            dve.tensor_copy(idx_u[:, 0, :], idx_all[:, 0:TOPK]).then_inc(idx_u_staged, 1)

            def weigh(n, par):
                dve.wait_ge(gelu_done, n + 1)
                dve.tensor_tensor(act_g[:, par, :], hid_g[:, par, :], gate_all[:, cols(n, TOPK)], ALU.mult).then_inc(act_ready, 1)

            def add_unit(n, par, b):
                dve.wait_ge(pick_free, RING + TOPK * (n + 1))
                r = res[:, bass.ds(b, 1), :].rearrange("p o d -> p (o d)")
                dve.tensor_tensor(r, r, bank[:, 4 * par:4 * par + 2, :].rearrange("p b n -> p (b n)"), ALU.add).then_inc(f_free, 1)

            def unit(n, par, b, b_added, has_1, has_2):
                for k in range(TOPK):
                    s = k % RING
                    if k == 3:
                        if has_1:
                            weigh(n - 1, 1 - par)
                        if has_2:
                            add_unit(n - 2, par, b_added)
                        dve.tensor_copy(idx_v[:, par, :], idx_all[:, cols(n, TOPK)]).then_inc(idx_v_staged, 1)
                        dve.tensor_copy(idx_u[:, 1 - par, :], idx_all[:, cols(n + 1, TOPK)]).then_inc(idx_u_staged, 1)
                    dve.wait_ge(u_loaded[s], 16 * (2 * n + k // RING + 1))
                    if has_1 or k >= 2:
                        dve.wait_ge(u_free, TOPK * n + (RING + k - 1))
                    dot = dve.scalar_tensor_tensor(products[:, k % 2, :], u_ring[:, s, :], 1.0, x1_all[:, bass.ds(b, 1), :].rearrange("p o d -> p (o d)"),
                                                   ALU.mult, ALU.mult, accum_out=hid[:, par, k:k + 1])
                    dot.then_inc(u_free, 1)

            unit(0, 0, 0, 0, False, False)
            unit(1, 1, 0, 0, True, False)
            with dve.Fori(1, UNITS // 2) as i:
                blk = dve.snap(i // 4)
                blk_added = dve.snap((i - 1) // 4)
                unit(2 * i, 0, blk, blk_added, True, True)
                unit(2 * i + 1, 1, blk, blk_added, True, True)
            weigh(UNITS - 1, 1)
            add_unit(UNITS - 2, 0, BLOCKS - 1)
            dve.wait_ge(f_free, 2 + UNITS - 1)
            add_unit(UNITS - 1, 1, BLOCKS - 1)
            dve.wait_ge(f_free, 2 + UNITS)
            dve.wait_ge(ln_loaded, 96)
            steps = Steps(dve, dve_e, dve_passed)
            def norm_out_pair(i):
                steps.at(2 * LN_LINKS * i)
                for par in range(2):
                    n = 2 * i + par

                    def slot_free():
                        need(dve, out_stored[par], 16 * i)

                    layer_norm(steps, 2 * BLOCKS + n, res[:, bass.ds(n, 1), :].rearrange("p o d -> p (o d)"),
                               normed[:, par, :], slot_free).then_inc(out_ready, 1)

            peeled(dve, BLOCKS // 2, norm_out_pair)


def kernel(**inputs):
    import numpy as _np
    import concourse.bacc as _bacc
    from concourse import mybir as _mybir
    from concourse.bass_utils import run_bass_kernel_spmd as _run

    a = {k: _np.asarray(v) for k, v in inputs.items()}
    w_in = a["w_in"][0]
    laid = {
        "x": a["x"].reshape(SEQ, D),
        "ln0_g": a["ln0_g"], "ln0_b": a["ln0_b"],
        "w_in_chunks": w_in[:, :12 * P].reshape(DCH, P, 12, P).transpose(2, 1, 0, 3),
        "w_v": w_in[:, 12 * P:],
        "pool_w": a["pool_w"][0],
        "pool_b": a["pool_b"][0].T,
        "pool_scale": a["pool_scale"][0].reshape(GROUPS, P).T,
        "w_out": a["w_out"][0],
        "ln1_g": a["ln1_g"][0], "ln1_b": a["ln1_b"][0],
        "wq_chunks": a["peer_wq"][0].reshape(DCH, P, 16, P).transpose(2, 1, 0, 3),
        "keys_t": a["peer_sub_keys"][0].transpose(0, 2, 1),
        "peer_u": a["peer_u"][0], "peer_v": a["peer_v"][0],
        "ln2_g": a["ln2_g"][0], "ln2_b": a["ln2_b"][0],
    }
    nc = _bacc.Bacc("TRN2", target_bir_lowering=False, num_devices=1)
    arrays, args = {}, []
    for name, v in laid.items():
        v = _np.ascontiguousarray(v)
        arrays[f"in_{name}"] = v
        args.append(nc.dram_tensor(f"in_{name}", v.shape, _mybir.dt.from_np(v.dtype), kind="ExternalInput").ap())
    o = nc.dram_tensor("out_0", (SEQ, D), F32, kind="ExternalOutput").ap()
    layer_kernel(nc, *args, o)
    r = _run(nc, [arrays], core_ids=[0])
    return r.results[0]["out_0"].reshape(a["x"].shape)
```

```python
import math
from contextlib import ExitStack

import concourse.bass as bass
from concourse import mybir

F32 = mybir.dt.float32
BF16 = mybir.dt.bfloat16
U32 = mybir.dt.uint32
ALU = mybir.AluOpType
ACT = mybir.ActivationFunctionType
AX = mybir.AxisListType

P = 128
SEQ = 1024
D = 1024
BLOCKS = SEQ // P
DCH = D // P
HALF = 512
POOL_WINDOWS = (2, 4, 8, 16)
GROUPS = len(POOL_WINDOWS)
HEADS = 8
HEAD_DIM = 64
HALVES = 2
PER_HALF = HEADS // HALVES
PEER_HEADS = 8
N_KEYS = 128
TOPK = 16
PICKS = PEER_HEADS * TOPK
UNITS = BLOCKS * PEER_HEADS
GATHERED = BLOCKS // 2
G_UNITS = GATHERED * PEER_HEADS
DENSE = BLOCKS - GATHERED
DT = DENSE * P
TILES = N_KEYS
TILE_GROUP = 4
TILE_GROUPS = TILES // TILE_GROUP
assert TILE_GROUPS == G_UNITS and DT == 512
OUTS = 2 * DENSE
OUT_RING = 4
BATCH = 16
BATCHES = DT // BATCH
BLOCK_BATCHES = P // BATCH
LN_EPS = 1e-5
ALPHA = 2.0 ** 0.25
CAP_OPEN = 3.0e38
CAP_SHUT = -1.0e30
LOWEST = -3.0e38
U_RING = 4
V_RING = 8
ROW_LEN = [TOPK // (a + 1) for a in range(TOPK)]
ROW_AT = [sum(ROW_LEN[:a]) for a in range(TOPK)]
CANDS = sum(ROW_LEN)


def need(engine, semaphore, value):
    if isinstance(value, int) and value <= 0:
        return
    engine.wait_ge(semaphore, value)


def peeled(engine, count, body):
    body(0)
    with engine.Fori(1, count) as i:
        body(i)


class Steps:

    def __init__(self, engine, semaphore, passed=None):
        self.engine, self.semaphore, self.passed, self.base, self.k = engine, semaphore, passed, 0, 0

    def at(self, base):
        self.base, self.k = base, 0

    def link(self, instruction):
        self.k += 1
        instruction.then_inc(self.semaphore, 1)
        self.engine.wait_ge(self.semaphore, self.base + self.k)
        if self.passed is not None:
            self.engine.sem_inc(self.passed, 1)


def layer_kernel(nc, x, ln0_g, ln0_b, w_in_chunks, w_v, pool_w, pool_b, pool_scale, w_out,
                 ln1_g, ln1_b, wq_chunks, keys_t, peer_u, peer_v, u_tiles, ln2_g, ln2_b, out):
    x_blocks = x.rearrange("(b p) d -> b p d", p=P)
    out_blocks = out.rearrange("(b p) d -> b p d", p=P)
    h0_dram = nc.dram_tensor("h0_scratch", (BLOCKS, P, D), F32).ap()
    g_dram = nc.dram_tensor("gates_scratch", (TILES, P, DT), F32).ap()
    v_tiles = peer_v.rearrange("(j e) d -> j e d", e=P)
    x1_dram = nc.dram_tensor("x1_scratch", (BLOCKS, P, D), F32).ap()

    ctx = ExitStack()
    with ctx:
        def sb(name, shape, dt=F32):
            return ctx.enter_context(nc.sbuf_tensor(name, shape, dt))

        def sem(name):
            return ctx.enter_context(nc.semaphore(name))

        KIB = 256
        arena = sb("arena", [P, 196 * KIB])

        def region(kib, cols):
            return arena[:, int(kib * KIB):int(kib * KIB) + cols]

        hT = region(0, DCH * SEQ).rearrange("p (c t) -> p c t", c=DCH)
        act_ring = hT[:, :, 0:DT]
        uqk = region(32, 12 * SEQ).rearrange("p (m t) -> p m t", m=12)
        x1_all = region(32, BLOCKS * D).rearrange("p (b d) -> p b d", b=BLOCKS)
        wo = region(80, DCH * D).rearrange("p (c d) -> p c d", c=DCH)
        wv = region(80, DCH * HALF).rearrange("p (c d) -> p c d", c=DCH)
        res = region(80, BLOCKS * D).rearrange("p (b d) -> p b d", b=BLOCKS)
        v_all = region(112, BLOCKS * HALF).rearrange("p (b d) -> p b d", b=BLOCKS)
        w_ring = region(128, 4 * D).rearrange("p (s c n) -> p s c n", s=4, c=DCH)
        pick_cols = region(48, 3 * DT).rearrange("p (r t) -> p r t", r=3)
        pick_rows = region(72.5, 3 * DT).rearrange("p (r t) -> p r t", r=3)
        key1_hot = region(48, 2 * BATCH * P).rearrange("p (s t n) -> p s t n", s=2, t=BATCH)
        key2_hot = region(176, 2 * BATCH * P).rearrange("p (s t n) -> p s t n", s=2, t=BATCH)
        gates = region(112, N_KEYS * P).rearrange("p (n t) -> p n t", n=N_KEYS)
        u_ring = region(48, U_RING * D).rearrange("p (s d) -> p s d", s=U_RING)
        v_ring = region(112, V_RING * D).rearrange("p (s d) -> p s d", s=V_RING)
        ut_ring = region(144, 2 * D).rearrange("p (s c e) -> p s c e", s=2, c=DCH)
        vt_ring = region(152, 8 * D).rearrange("p (s d) -> p s d", s=8)
        g_ring = region(184, 4 * DT).rearrange("p (s t) -> p s t", s=4)
        gelu_ring = region(192, 2 * DT).rearrange("p (s t) -> p s t", s=2)
        ln2_rows = region(72, 2 * D).rearrange("p (r d) -> p r d", r=2)
        ln_rows = region(144, 2 * D).rearrange("p (r d) -> p r d", r=2)
        xin = region(152, 2 * D).rearrange("p (s d) -> p s d", s=2)
        qpeer = region(152, 2 * D).rearrange("p (s d) -> p s d", s=2)
        normed = region(160, 2 * D).rearrange("p (s d) -> p s d", s=2)
        h0_back = region(152, D)
        x1_pre = region(156, D)
        q_pad = region(168, HEADS * P).rearrange("p (h q) -> p h q", h=HEADS)
        sp = region(172, HEADS * P).rearrange("p (h q) -> p h q", h=HEADS)
        sp_sum = region(176, HEADS * P).rearrange("p (h q) -> p h q", h=HEADS)
        attn = region(180, HEADS * P).rearrange("p (h q) -> p h q", h=HEADS)
        soft = region(184, HEADS * P).rearrange("p (h q) -> p h q", h=HEADS)
        mix_t = region(188, DCH * P).rearrange("p (c q) -> p c q", c=DCH)
        k_stage = region(192, 4 * P).rearrange("p (c k) -> p c k", c=4)
        o_stage = region(194, HALF)
        win_a = region(172, SEQ)
        win_b = region(176, SEQ)
        match = region(168, BLOCKS * TOPK * CANDS).rearrange("p (g c) -> p g c", c=CANDS)
        idx_all = region(64, UNITS * TOPK + TOPK).bitcast(U32)
        gate_all = region(68.25, UNITS * TOPK)
        key_work = region(72.5, BLOCKS * N_KEYS).rearrange("p (b n) -> p b n", b=BLOCKS)

        def small(name, shape, dt=F32):
            return sb(name, shape, dt)

        ident = small("ident", [P, P])
        neg_tri = small("neg_tri", [P, P])
        neg_ones = small("neg_ones", [P, P])
        cap = small("cap", [P, P])
        keys_sb = small("keys_sb", [P, 2, N_KEYS])
        pool_w_sb = small("pool_w_sb", [P, GROUPS, P])
        pool_bs = small("pool_bs", [P, 2, GROUPS])
        kind_scale = small("kind_scale", [P, 3])
        inv_count = small("inv_count", [P, TOPK])
        head_cols = small("head_cols", [P, TOPK])
        iota_k = small("iota_k", [P, N_KEYS])
        stats = small("stats", [P, 2, 6])
        mean_var = small("mean_var", [P, 2])
        eps_col = small("eps_col", [P, 1])
        one_col = small("one_col", [P, 1])
        zero_row = small("zero_row", [1, P])
        lnv = small("lnv", [P, 1])
        rstd0 = small("rstd0", [P, 1])
        newton = small("newton", [P, 1])
        rstd = small("rstd", [P, 1])
        top_s = region(112, 2 * BLOCKS * TOPK).rearrange("p (h b k) -> p h b k", h=2, b=BLOCKS)
        top_i = region(113, 2 * BLOCKS * TOPK).bitcast(U32).rearrange("p (h b k) -> p h b k", h=2, b=BLOCKS)
        top_if = region(114, 2 * BLOCKS * TOPK).rearrange("p (h b k) -> p h b k", h=2, b=BLOCKS)
        cand = region(115, BLOCKS * CANDS).rearrange("p (b k) -> p b k", b=BLOCKS)
        cand_e = region(116.75, BLOCKS * CANDS).rearrange("p (b k) -> p b k", b=BLOCKS)
        cand_w = region(118.5, BLOCKS * CANDS).rearrange("p (b k) -> p b k", b=BLOCKS)
        best_s = region(120.25, BLOCKS * TOPK).rearrange("p (b k) -> p b k", b=BLOCKS)
        best_p = region(120.75, BLOCKS * TOPK).bitcast(U32).rearrange("p (b k) -> p b k", b=BLOCKS)
        best_pf = region(121.25, BLOCKS * TOPK).rearrange("p (b k) -> p b k", b=BLOCKS)
        gate_sum = small("gate_sum", [P, BLOCKS])
        idx_u = small("idx_u", [P, 2, TOPK], U32)
        idx_v = small("idx_v", [P, 2, TOPK], U32)
        hid = small("hid", [P, 2, TOPK])
        hid_g = small("hid_g", [P, 2, TOPK])
        act_g = small("act_g", [P, 2, TOPK])

        bank = ctx.enter_context(nc.psum_tensor("bank", [P, 8, HALF], F32))
        z = bank[:, 0:2, :]
        o_ps = bank[:, 2, :]
        oT_ps = bank[:, 3, :].rearrange("p (c q) -> p c q", c=4)
        y_ps = bank[:, 4:6, :].rearrange("p b n -> p (b n)")
        xT_ps = bank[:, 6:8, :].rearrange("p b (c q) -> p (b c) q", q=P)

        consts = sem("consts_made")
        const_step = sem("const_step")
        ln_loaded = sem("ln_loaded")
        small_loaded = sem("small_weights_loaded")
        x_loaded = [sem(f"x_loaded{i}") for i in range(2)]
        x_free = sem("x_slot_free")
        h0_ready = sem("h0_ready")
        h0_stored = [sem(f"h0_stored{i}") for i in range(2)]
        h0_transposed = sem("h0_transposed")
        h0t_copied = sem("h0t_copied")
        w_loaded = [sem(f"w_loaded{i}") for i in range(4)]
        wv_loaded = sem("wv_loaded")
        wo_loaded = sem("wo_loaded")
        proj_done = sem("proj_done")
        proj_copied = sem("proj_copied")
        v_done = sem("v_done")
        v_copied = sem("v_copied")
        pooled = sem("pooled")
        pool_mm = sem("pool_mm_done")
        pool_mixed = sem("pool_mixed")
        var_ready = sem("var_ready")
        rstd0_ready = sem("rstd0_ready")
        act_step = sem("act_step")
        pool_passed = sem("pool_passed_wait")
        dve_passed = sem("dve_passed_wait")
        dve_a = sem("dve_step_a")
        dve_b = sem("dve_step_b")
        dve_c = sem("dve_step_c")
        dve_d = sem("dve_step_d")
        dve_e = sem("dve_step_e")
        q_staged = sem("q_staged")
        k_staged = sem("k_staged")
        z_done = sem("z_done")
        z_capped = sem("z_capped")
        ln_ready = sem("ln_ready")
        sp_ready = sem("sp_ready")
        sum_ready = sem("sum_ready")
        c_done = sem("c_done")
        a_ready = sem("a_ready")
        av_done = sem("av_done")
        o_copied = sem("o_copied")
        o_transposed = sem("o_transposed")
        mix_copied = sem("mix_copied")
        mixp_staged = sem("mixp_staged")
        y_done = sem("y_done")
        y_read = sem("y_read")
        h0_reloaded = sem("h0_reloaded")
        x1_ready = sem("x1_ready")
        x1_transposed = sem("x1_transposed")
        x1t_copied = sem("x1t_copied")
        x1_stored = sem("x1_stored")
        wq_done = sem("wq_done")
        qp_copied = sem("qp_copied")
        score_ready = sem("score_ready")
        score_free = sem("score_bank_free")
        gate_in = sem("gate_in_ready")
        gate_exp = sem("gate_exp_ready")
        x1_back = sem("x1_back")
        res_init = sem("residual_scaled")
        picks_split = sem("picks_split")
        picks_turned = sem("picks_turned")
        picks_kept = sem("picks_kept")
        key1_gated = sem("key1_hot_gated")
        key1_ready = sem("key1_hot_ready")
        key2_ready = sem("key2_hot_ready")
        gates_done = sem("gates_done")
        gates_copied = sem("gates_copied")
        gates_stored = sem("gates_stored")
        ut_loaded = [sem(f"u_tile_loaded{i}") for i in range(2)]
        vt_loaded = [sem(f"v_tile_loaded{i}") for i in range(2)]
        gt_loaded = [sem(f"gate_tile_loaded{i}") for i in range(4)]
        hid_done = sem("hidden_tile_done")
        hid_gelu = sem("hidden_tile_gelu")
        act_made = sem("act_tile_made")
        out_done = sem("out_bank_done")
        out_added = sem("out_bank_added")
        idx_u_staged = sem("idx_u_staged")
        idx_v_staged = sem("idx_v_staged")
        u_loaded = [sem(f"u_loaded{i}") for i in range(U_RING)]
        v_loaded = [sem(f"v_loaded{i}") for i in range(V_RING)]
        u_free = sem("u_slot_free")
        v_free = sem("v_slot_free")
        gelu_done = sem("gelu_done")
        act_ready = sem("act_ready")
        out_ready = sem("out_ready")
        out_stored = [sem(f"out_stored{i}") for i in range(2)]

        block = ctx.enter_context(nc.Block())

        def block_of(ap, n):
            return ap[bass.ds(n, 1)].rearrange("o p d -> p (o d)")

        def cols(n, width=P):
            return bass.ds(n * width, width)

        def pairs_before(b):
            return b * (b + 1) // 2

        def first_step(engine, b):
            return engine.snap(engine.snap((b - 1) * (b + 2) // 2) + 1)

        def key_block(b, i):
            if isinstance(b, int):
                return b - i
            return nc.s_assert_within(b - i, 0, BLOCKS - 1, skip_runtime_bounds_check_because="i runs from 0 to b")

        @block.sync
        def _(sync):
            def load_ln(g, b, rows=ln_rows):
                sync.dma_start(rows[:, 0, :], g.partition_broadcast(P)).then_inc(ln_loaded, 16)
                sync.dma_start(rows[:, 1, :], b.partition_broadcast(P)).then_inc(ln_loaded, 16)

            load_ln(ln0_g, ln0_b)
            with sync.Fori(0, BLOCKS // 2) as i:
                for par in range(2):
                    n = 2 * i + par
                    sync.wait_ge(x_free, n + 1)
                    sync.dma_start(xin[:, par, :], block_of(x_blocks, n)).then_inc(x_loaded[par], 16)
            with sync.Fori(1, 3) as kind:
                for s in range(4):
                    sync.wait_ge(proj_done, 4 * kind + s - 3)
                    sync.dma_start(w_ring[:, s], w_in_chunks[bass.ds(4 * kind + s, 1)].rearrange("o p c n -> p (o c) n")).then_inc(w_loaded[s], 16)
            sync.wait_ge(h0_ready, BLOCKS)
            load_ln(ln1_g, ln1_b)
            for s in range(4):
                sync.wait_ge(proj_done, 9 + s)
                sync.dma_start(w_ring[:, s], wq_chunks[s]).then_inc(w_loaded[s], 16)
            sync.wait_ge(v_done, BLOCKS)
            sync.dma_start(wo, w_out.rearrange("(c p) d -> p c d", p=P)).then_inc(wo_loaded, 16)
            for par in range(2):
                sync.wait_ge(h0_stored[par], 16 * (BLOCKS // 2))
            def stage_c_block(b):
                need(sync, y_read, b)
                sync.dma_start(h0_back, block_of(h0_dram, b)).then_inc(h0_reloaded, 16)
                sync.wait_ge(x1_ready, b + 1)
                sync.dma_start(block_of(x1_dram, b), normed[:, 0, :]).then_inc(x1_stored, 16)

            peeled(sync, BLOCKS, stage_c_block)
            sync.wait_ge(x1_stored, 16 * BLOCKS)
            sync.wait_ge(wq_done, 1)
            sync.dma_start(x1_all, x1_dram.rearrange("b p d -> p b d")).then_inc(x1_back, 16)
            with sync.Fori(1, 4) as i:
                for s in range(4):
                    sync.wait_ge(wq_done, 4 * i + s - 3)
                    sync.dma_start(w_ring[:, s], wq_chunks[bass.ds(4 * i + s, 1)].rearrange("o p c n -> p (o c) n")).then_inc(w_loaded[s], 16)
            with sync.Fori(0, DENSE) as b:
                sync.wait_ge(gates_copied, BLOCK_BATCHES * (b + 1))
                sync.dma_start(g_dram[:, :, cols(b)].rearrange("n p t -> p n t"), gates).then_inc(gates_stored, 16)
            sync.wait_ge(gates_stored, 16 * DENSE)
            load_ln(ln2_g, ln2_b, ln2_rows)

            def load_v_group(g, par):
                tiles = v_tiles[0:TILE_GROUP] if isinstance(g, int) and g == 0 else v_tiles[bass.ds(g * TILE_GROUP, TILE_GROUP)]
                sync.dma_start(vt_ring[:, TILE_GROUP * par:TILE_GROUP * (par + 1), :], tiles.rearrange("j e d -> e j d")).then_inc(vt_loaded[par], 16)

            load_v_group(0, 0)
            load_v_group(1, 1)
            with sync.Fori(1, TILE_GROUPS // 2) as i:
                for par in range(2):
                    g = 2 * i + par
                    sync.wait_ge(out_done, OUTS * g)
                    load_v_group(g, par)
            with sync.Fori(0, BLOCKS // 2) as i:
                for par in range(2):
                    n = 2 * i + par
                    sync.wait_ge(out_ready, n + 1)
                    sync.dma_start(block_of(out_blocks, n), normed[:, par, :]).then_inc(out_stored[par], 16)
            for par in range(2):
                sync.wait_ge(out_stored[par], 16 * (BLOCKS // 2))

        @block.gpsimd
        def _(pool):
            pool.memset(ident[:], 0.0)
            pool.memset(neg_tri[:], -1.0)
            pool.memset(neg_ones[:], -1.0)
            pool.memset(cap[:], CAP_OPEN)
            pool.memset(kind_scale[:], 1.0)
            pool.memset(eps_col[:], LN_EPS)
            pool.memset(one_col[:], 1.0)
            pool.memset(zero_row[:], 0.0)
            pool.memset(q_pad, 0.0)
            pool.memset(idx_u[:], 0)
            pool.iota(iota_k[:], pattern=[[1, N_KEYS]], base=0, channel_multiplier=0, allow_small_or_imprecise_dtypes=True)
            pool.iota(inv_count[:], pattern=[[1, TOPK]], base=1, channel_multiplier=0, allow_small_or_imprecise_dtypes=True).then_inc(const_step, 1)
            pool.wait_ge(const_step, 1)
            pool.affine_select(out=ident[:], in_=ident[:], compare_op=ALU.not_equal, fill=1.0, base=0,
                               pattern=[[-1, P]], channel_multiplier=1)
            pool.affine_select(out=neg_tri[:], in_=neg_tri[:], compare_op=ALU.is_ge, fill=0.0, base=0,
                               pattern=[[-1, P]], channel_multiplier=1)
            pool.affine_select(out=cap[:], in_=cap[:], compare_op=ALU.is_gt, fill=CAP_SHUT, base=0,
                               pattern=[[1, P]], channel_multiplier=-1)
            pool.memset(kind_scale[:, 1:2], HEAD_DIM ** -0.5).then_inc(consts, 1)
            with pool.Fori(0, BLOCKS // 2) as i:
                for par in range(2):
                    n = 2 * i + par
                    pool.wait_ge(h0_ready, n + 1)
                    pool.dma_start(block_of(h0_dram, n), normed[:, par, :]).then_inc(h0_stored[par], 16)

            def begin_block(b, n):
                need(pool, z_done, 2 * n)
                pool.tensor_copy(k_stage, uqk[:, 8:12, cols(b)]).then_inc(k_staged, 1)
                need(pool, c_done, 2 * n)
                pool.sem_inc(pool_passed, 1)
                for c in range(HALVES):
                    pool.memset(sp_sum[:, c * PER_HALF:(c + 1) * PER_HALF], 0.0).then_inc(sum_ready, 1)

            def later_keys(b, i, n):
                pool.wait_ge(z_done, 2 * n)
                pool.tensor_copy(k_stage, uqk[:, 8:12, cols(key_block(b, i))]).then_inc(k_staged, 1)
                for c in range(HALVES):
                    hs = slice(c * PER_HALF, (c + 1) * PER_HALF)
                    pool.wait_ge(sum_ready, 2 * n + c - 1)
                    pool.wait_ge(sp_ready, 2 * n + c - 1)
                    pool.wait_ge(c_done, 2 * n + c - 1)
                    pool.tensor_tensor(sp_sum[:, hs], sp_sum[:, hs], sp[:, hs], ALU.add).then_inc(sum_ready, 1)

            pool.wait_ge(proj_copied, 12)
            pool.wait_ge(pool_mixed, GROUPS)
            begin_block(0, 0)
            with pool.Fori(1, BLOCKS) as b:
                first = first_step(pool, b)
                begin_block(b, first)
                with pool.Fori(1, b + 1) as i:
                    later_keys(b, i, pool.snap(first + i))

            pool.wait_ge(x1_back, 16)
            pool.wait_ge(y_done, BLOCKS)
            for b in range(BLOCKS):
                pool.tensor_scalar(res[:, b, :], x1_all[:, b, :], ALPHA, 0.0, ALU.mult, ALU.add).then_inc(res_init, 1)

            def gate_batch(t, par):
                pool.wait_ge(key1_ready, t + 1)
                pool.tensor_tensor(key1_hot[:, par], key1_hot[:, par],
                                   pick_rows[:, 2, bass.ds(t * BATCH, BATCH)].unsqueeze(2).broadcast_to([P, BATCH, N_KEYS]),
                                   ALU.mult).then_inc(key1_gated, 1)

            with pool.Fori(0, BATCHES // 2) as i:
                for par in range(2):
                    gate_batch(2 * i + par, par)

            pool.wait_ge(gates_stored, 16 * DENSE)

            def gathers(u_unit, u_par, v_unit, v_par):
                if u_unit is not None:
                    pool.wait_ge(idx_u_staged, u_unit + 1)
                if v_unit is not None:
                    pool.wait_ge(idx_v_staged, v_unit + 1)
                for k in range(TOPK):
                    if u_unit is not None:
                        pool.wait_ge(u_free, TOPK * u_unit + k + 1)
                        pool.sem_inc(pool_passed, 1)
                        pool.indirect_dma_start(u_ring[:, k % U_RING, :], None, peer_u,
                                                bass.IndirectOffsetOnAxis(ap=idx_u[:, u_par, k:k + 1], axis=0)).then_inc(u_loaded[k % U_RING], 16)
                    if v_unit is not None:
                        pool.wait_ge(v_free, TOPK * v_unit + k + 1)
                        pool.sem_inc(pool_passed, 1)
                        pool.indirect_dma_start(v_ring[:, k % V_RING, :], None, peer_v,
                                                bass.IndirectOffsetOnAxis(ap=idx_v[:, v_par, k:k + 1], axis=0)).then_inc(v_loaded[k % V_RING], 16)

            gathers(0, 0, None, 0)
            gathers(1, 1, 0, 0)
            with pool.Fori(1, G_UNITS // 2) as i:
                gathers(2 * i, 0, 2 * i - 1, 1)
                gathers(2 * i + 1, 1, 2 * i, 0)
            gathers(None, 0, G_UNITS - 1, 1)

        @block.scalar
        def _(act):
            def rsqrt_seed(n):
                act.wait_ge(var_ready, n + 1)
                act.activation(lnv[:], mean_var[:, 1:2], ACT.Ln, bias=eps_col[:]).then_inc(act_step, 1)
                act.wait_ge(act_step, n + 1)
                act.activation(rstd0[:], lnv[:], ACT.Exp, scale=-0.5).then_inc(rstd0_ready, 1)

            act.preload_act_table_set("natural_log_exp_and_others")
            for s in range(4):
                act.dma_start(w_ring[:, s], w_in_chunks[s]).then_inc(w_loaded[s], 16)
            act.dma_start(pool_w_sb[:], pool_w.rearrange("g c d -> c g d")).then_inc(small_loaded, 16)
            act.dma_start(pool_bs[:, 0, :], pool_b).then_inc(small_loaded, 16)
            act.dma_start(pool_bs[:, 1, :], pool_scale).then_inc(small_loaded, 16)
            act.dma_start(keys_sb[:], keys_t.rearrange("h c n -> c h n")).then_inc(small_loaded, 16)
            act.dma_start(wv, w_v.rearrange("(c p) n -> p c n", p=P)).then_inc(wv_loaded, 16)
            act.wait_ge(consts, 1)
            with act.Fori(0, BLOCKS // 2) as i:
                for par in range(2):
                    n = 2 * i + par
                    rsqrt_seed(n)
                    act.wait_ge(h0_transposed, n + 1)
                    act.activation(hT[:, :, cols(n)], bank[:, 2 * par:2 * par + 2, :].rearrange("p b (c q) -> p (b c) q", q=P),
                                   ACT.Copy).then_inc(h0t_copied, 1)
            with act.Fori(0, 3) as kind:
                for s in range(4):
                    act.wait_ge(proj_done, 4 * kind + s + 1)
                    act.activation(uqk[:, bass.ds(4 * kind + s, 1), :].rearrange("p o t -> p (o t)"),
                                   bank[:, 2 * s:2 * s + 2, :].rearrange("p b n -> p (b n)"), ACT.Copy,
                                   scale=kind_scale[:, bass.ds(kind, 1)]).then_inc(proj_copied, 1)
            for b in range(BLOCKS):
                act.wait_ge(v_done, b + 1)
                act.activation(v_all[:, b, :], bank[:, b, :], ACT.Copy).then_inc(v_copied, 1)

            def stage_queries(b, n):
                need(act, z_done, 2 * n)
                act.activation(q_pad[0:64, 0:HEADS:2, :], uqk[0:64, 4:8, cols(b)], ACT.Copy)
                act.activation(q_pad[64:128, 1:HEADS:2, :], uqk[64:128, 4:8, cols(b)], ACT.Copy).then_inc(q_staged, 1)

            def log_terms(n, c, steps_at, diagonal_of=None):
                hs = slice(c * PER_HALF, (c + 1) * PER_HALF)
                if diagonal_of is None:
                    act.wait_ge(z_done, 2 * n + c + 1)
                else:
                    act.wait_ge(z_capped, 2 * diagonal_of + c + 1)
                need(act, sp_ready, 2 * n + c - 1)
                act.activation(soft[:, hs], z[:, c, :].rearrange("p (h q) -> p h q", q=P), ACT.Abs).then_inc(act_step, 1)
                act.wait_ge(act_step, steps_at + 2 * c + 1)
                act.activation(soft[:, hs], soft[:, hs], ACT.Exp, scale=-1.0).then_inc(act_step, 1)
                act.wait_ge(act_step, steps_at + 2 * c + 2)
                act.activation(soft[:, hs], soft[:, hs], ACT.Ln, bias=one_col[:]).then_inc(ln_ready, 1)

            def weights(n, c):
                hs = slice(c * PER_HALF, (c + 1) * PER_HALF)
                act.wait_ge(c_done, 2 * n + c + 1)
                need(act, av_done, 2 * n + c - 1)
                act.activation(attn[:, hs], z[:, c, :].rearrange("p (h q) -> p h q", q=P), ACT.Exp).then_inc(a_ready, 1)

            def attention_out(b, n_end):
                act.wait_ge(av_done, 2 * n_end)
                act.activation(o_stage, o_ps, ACT.Copy).then_inc(o_copied, 1)
                act.activation(mix_t[:, 0:4, :], uqk[:, 0:4, cols(b)], ACT.Copy).then_inc(mixp_staged, 1)

            def attention_transposed(b):
                act.wait_ge(o_transposed, b + 1)
                act.activation(mix_t[:, 4:8, :], oT_ps, ACT.Copy).then_inc(mix_copied, 1)

            def x1_transpose_out(b):
                act.wait_ge(x1_transposed, b + 1)
                act.activation(hT[:, :, cols(b)], xT_ps, ACT.Copy).then_inc(x1t_copied, 1)

            stage_queries(0, 0)
            act.wait_ge(pool_mixed, GROUPS)
            log_terms(0, 0, BLOCKS, 0)
            log_terms(0, 1, BLOCKS, 0)
            weights(0, 0)
            weights(0, 1)
            with act.Fori(1, BLOCKS) as b:
                first = first_step(act, b)
                steps_at = 4 * first + BLOCKS + b - 1
                stage_queries(b, first)
                attention_out(b - 1, first)
                log_terms(first, 0, steps_at, b)
                attention_transposed(b - 1)
                log_terms(first, 1, steps_at, b)
                weights(first, 0)
                act.wait_ge(var_ready, BLOCKS + b)
                act.activation(lnv[:], mean_var[:, 1:2], ACT.Ln, bias=eps_col[:]).then_inc(act_step, 1)
                act.wait_ge(act_step, 4 * first + BLOCKS + b + 4)
                act.activation(rstd0[:], lnv[:], ACT.Exp, scale=-0.5).then_inc(rstd0_ready, 1)
                with act.Fori(1, b + 1) as i:
                    n = act.snap(first + i)
                    log_terms(n, 0, 4 * n + BLOCKS + b)
                    weights(n - 1, 1)
                    log_terms(n, 1, 4 * n + BLOCKS + b)
                    weights(n, 0)
                weights(first + b, 1)
                x1_transpose_out(b - 1)
            attention_out(BLOCKS - 1, pairs_before(BLOCKS))
            attention_transposed(BLOCKS - 1)
            total = 4 * pairs_before(BLOCKS) + BLOCKS + BLOCKS - 1
            act.wait_ge(var_ready, 2 * BLOCKS)
            act.activation(lnv[:], mean_var[:, 1:2], ACT.Ln, bias=eps_col[:]).then_inc(act_step, 1)
            act.wait_ge(act_step, total + 1)
            act.activation(rstd0[:], lnv[:], ACT.Exp, scale=-0.5).then_inc(rstd0_ready, 1)
            x1_transpose_out(BLOCKS - 1)
            def gate_exps(h):
                act.wait_ge(gate_in, h + 1)
                act.activation(best_s, best_s, ACT.Exp).then_inc(gate_exp, 1)

            def query_copies(i):
                for s in range(4):
                    act.wait_ge(wq_done, 4 * i + s + 1)
                    act.activation(qpeer[:, s % 2, :], bank[:, 2 * (s % 2):2 * (s % 2) + 2, :].rearrange("p b n -> p (b n)"),
                                   ACT.Copy).then_inc(qp_copied, 1)
                    if s % 2 and not (isinstance(i, int) and s == 1):
                        gate_exps(2 * i + s // 2 - 1)

            peeled(act, 4, query_copies)
            gate_exps(PEER_HEADS - 1)

            for r in range(3):
                act.wait_ge(picks_turned, r + 1)
                act.activation(pick_rows[:, r, :], bank[:, r, :], ACT.Copy).then_inc(picks_kept, 1)
            def gates_block(b):
                need(act, gates_stored, 16 * b)
                for t in range(BLOCK_BATCHES):
                    act.wait_ge(gates_done, BLOCK_BATCHES * b + t + 1)
                    act.activation(gates[:, :, t * BATCH:(t + 1) * BATCH],
                                   bank[:, 4 * (t % 2):4 * (t % 2) + 4, :].rearrange("p b (t n) -> p n (b t)", n=N_KEYS), ACT.Copy).then_inc(gates_copied, 1)

            peeled(act, DENSE, gates_block)

            act.wait_ge(gates_stored, 16 * DENSE)

            def load_u_tile(j, s):
                act.dma_start(ut_ring[:, s], u_tiles[bass.ds(j, 1)].rearrange("o p c e -> p (o c) e")).then_inc(ut_loaded[s], 16)

            def load_gate_tile(j, s):
                act.dma_start(g_ring[:, s, :], g_dram[bass.ds(j, 1)].rearrange("o p t -> p (o t)")).then_inc(gt_loaded[s], 16)

            for j in range(2):
                load_u_tile(j, j)
                load_gate_tile(j, j)
            act.sem_inc(hid_gelu, 2)

            def unit_gelu(n, par):
                act.wait_ge(u_free, U_RING + TOPK * (n + 1))
                act.wait_ge(act_ready, n + 1)
                act.activation(hid_g[:, par, :], hid[:, par, :], ACT.Gelu).then_inc(gelu_done, 1)

            def hidden_tiles(g, par, last=False):
                for q in range(TILE_GROUP):
                    j = TILE_GROUP * g + q
                    act.wait_ge(act_made, j + 1)
                    if not (last and q >= TILE_GROUP - 2):
                        load_gate_tile(j + 2, (q + 2) % 4)
                    act.wait_ge(hid_done, j + 1)
                    act.activation(gelu_ring[:, q % 2, :], bank[:, q % 2, :], ACT.Gelu).then_inc(hid_gelu, 1)
                    if not (last and q >= TILE_GROUP - 2):
                        load_u_tile(j + 2, q % 2)
                unit_gelu(g, par)

            with act.Fori(0, TILE_GROUPS // 2 - 1) as i:
                for par in range(2):
                    hidden_tiles(2 * i + par, par)
            hidden_tiles(TILE_GROUPS - 2, 0)
            hidden_tiles(TILE_GROUPS - 1, 1, True)
            act.preload_act_table_set("natural_log_exp_and_others")
            with act.Fori(0, BLOCKS) as b:
                act.wait_ge(var_ready, 2 * BLOCKS + b + 1)
                act.activation(lnv[:], mean_var[:, 1:2], ACT.Ln, bias=eps_col[:]).then_inc(act_step, 1)
                act.wait_ge(act_step, total + 2 + b)
                act.activation(rstd0[:], lnv[:], ACT.Exp, scale=-0.5).then_inc(rstd0_ready, 1)

        @block.tensor
        def _(pe):
            pe.wait_ge(consts, 1)
            def transpose_pair(i):
                for par in range(2):
                    pe.wait_ge(h0_ready, 2 * i + par + 1)
                    need(pe, h0t_copied, 2 * i)
                    for c in range(DCH):
                        mm = pe.transpose(bank[:, 2 * par + c // 4, cols(c % 4)], normed[:, par, cols(c)], ident[:])
                    mm.then_inc(h0_transposed, 1)

            peeled(pe, BLOCKS // 2, transpose_pair)
            pe.wait_ge(h0t_copied, BLOCKS)
            def project_chunks(kind):
                need(pe, proj_copied, 4 * kind)
                for s in range(4):
                    pe.wait_ge(w_loaded[s], 16 * (kind + 1))
                    for half in range(2):
                        for c in range(DCH):
                            mm = pe.matmul(bank[:, 2 * s + half, :], w_ring[:, s, c, :], hT[:, c, cols(half, HALF)],
                                           start=(c == 0), stop=(c == DCH - 1))
                    mm.then_inc(proj_done, 1)

            peeled(pe, 3, project_chunks)
            pe.wait_ge(wv_loaded, 16)
            pe.wait_ge(proj_copied, 12)
            for b in range(BLOCKS):
                for c in range(DCH):
                    mm = pe.matmul(bank[:, b, :], hT[:, c, cols(b)], wv[:, c, :], start=(c == 0), stop=(c == DCH - 1))
                mm.then_inc(v_done, 1)
            pe.wait_ge(small_loaded, 64)
            for g in range(GROUPS):
                pe.wait_ge(v_copied, 2 * g + 2)
                pe.wait_ge(pooled, g + 1)
                for half in range(2):
                    mm = pe.matmul(bank[:, 2 * g + half, :], pool_w_sb[:, g, :], uqk[:, g, cols(half, HALF)], start=True, stop=True)
                mm.then_inc(pool_mm, 1)
            pe.wait_ge(pool_mixed, GROUPS)

            def scores(n, c, diagonal_of=None):
                if c == 0:
                    pe.wait_ge(k_staged, n + 1)
                    if diagonal_of is not None:
                        pe.wait_ge(q_staged, diagonal_of + 1)
                need(pe, a_ready, 2 * n + c - 1)
                for hh in range(PER_HALF):
                    h = c * PER_HALF + hh
                    mm = pe.matmul(z[:, c, cols(hh)], k_stage[:, h // 2, :], q_pad[:, h, :], start=(hh == 0), stop=True, skip_group_check=True)
                mm.then_inc(z_done, 1)

            def sums(n, c, earlier=True):
                hs = slice(c * PER_HALF, (c + 1) * PER_HALF)
                pe.wait_ge(sp_ready, 2 * n + c + 1)
                mm = pe.matmul(z[:, c, :], neg_tri[:], sp[:, hs].rearrange("p h q -> p (h q)"), start=False, stop=True, skip_group_check=True)
                if earlier:
                    pe.wait_ge(sum_ready, 2 * n + c + 1)
                    mm = pe.matmul(z[:, c, :], neg_ones[:], sp_sum[:, hs].rearrange("p h q -> p (h q)"), start=False, stop=True, skip_group_check=True)
                mm.then_inc(c_done, 1)

            def values(n, c, key):
                pe.wait_ge(a_ready, 2 * n + c + 1)
                for hh in range(PER_HALF):
                    h = c * PER_HALF + hh
                    mm = pe.matmul(o_ps[:, cols(h, HEAD_DIM)], attn[:, h, :], v_all[:, bass.ds(key, 1), cols(h, HEAD_DIM)].rearrange("p o d -> p (o d)"),
                                   start=False, stop=True, skip_group_check=True)
                mm.then_inc(av_done, 1)

            def clear_values(b):
                need(pe, o_copied, b)
                pe.matmul(o_ps[:, 0:P], zero_row[:], ident[0:1, :], start=True, stop=True, skip_group_check=True)

            def output_projection(b):
                pe.wait_ge(o_copied, b + 1)
                for c in range(4):
                    mm = pe.transpose(oT_ps[:, c, :], o_stage[:, cols(c)], ident[:])
                mm.then_inc(o_transposed, 1)
                pe.wait_ge(mixp_staged, b + 1)
                pe.wait_ge(mix_copied, b + 1)
                need(pe, y_read, b)
                for half in range(2):
                    for c in range(DCH):
                        mm = pe.matmul(y_ps[:, cols(half, HALF)], mix_t[:, c, :], wo[:, c, cols(half, HALF)], start=(c == 0), stop=(c == DCH - 1))
                mm.then_inc(y_done, 1)

            def x1_transposes(b):
                pe.wait_ge(x1_ready, b + 1)
                need(pe, x1t_copied, b)
                for c in range(DCH):
                    mm = pe.transpose(xT_ps[:, c, :], normed[:, 0, cols(c)], ident[:])
                mm.then_inc(x1_transposed, 1)

            scores(0, 0, 0)
            scores(0, 1, 0)
            clear_values(0)
            sums(0, 0, False)
            sums(0, 1)
            values(0, 0, 0)
            values(0, 1, 0)
            pe.wait_ge(wo_loaded, 16)
            with pe.Fori(1, BLOCKS) as b:
                first = first_step(pe, b)
                scores(first, 0, b)
                scores(first, 1, b)
                output_projection(b - 1)
                clear_values(b)
                sums(first, 0, False)
                with pe.Fori(1, b + 1) as i:
                    n = pe.snap(first + i)
                    scores(n, 0)
                    sums(n - 1, 1)
                    values(n - 1, 0, key_block(b, i - 1))
                    scores(n, 1)
                    sums(n, 0)
                    values(n - 1, 1, key_block(b, i - 1))
                last = pe.snap(first + b)
                sums(last, 1)
                x1_transposes(b - 1)
                values(last, 0, 0)
                values(last, 1, 0)
            output_projection(BLOCKS - 1)
            x1_transposes(BLOCKS - 1)
            pe.wait_ge(x1t_copied, BLOCKS)
            def query_chunks(i):
                for s in range(4):
                    par = s % 2
                    pe.wait_ge(w_loaded[s], 16 * (i + 4))
                    need(pe, qp_copied, 4 * i + s)
                    for half in range(2):
                        for c in range(DCH):
                            mm = pe.matmul(bank[:, 2 * par + half, :], w_ring[:, s, c, :], hT[:, c, cols(half, HALF)],
                                           start=(c == 0), stop=(c == DCH - 1))
                    mm.then_inc(wq_done, 1)
                    pe.wait_ge(qp_copied, 4 * i + s + 1)
                    pe.wait_ge(score_free, 4 * i + s + 1)
                    for b in range(BLOCKS):
                        mm = pe.matmul(bank[:, 4 + 2 * par + b // 4, cols(b % 4)], qpeer[:, par, cols(b)], keys_sb[:, s % 2, :], start=True, stop=True)
                    mm.then_inc(score_ready, 1)

            peeled(pe, 4, query_chunks)
            pe.wait_ge(picks_split, 1)
            pe.wait_ge(qp_copied, 16)
            for r in range(3):
                for b in range(DENSE):
                    mm = pe.transpose(bank[:, r, cols(b)], pick_cols[:, r, cols(b)], ident[:])
                mm.then_inc(picks_turned, 1)
            pe.wait_ge(picks_kept, 3)

            def gates_pair(i):
                for par in range(2):
                    pe.wait_ge(key1_gated, 2 * i + par + 1)
                    pe.wait_ge(key2_ready, 2 * i + par + 1)
                    need(pe, gates_copied, 2 * i + par - 1)
                    for t in range(BATCH):
                        mm = pe.matmul(bank[:, 4 * par + t // 4, cols(t % 4)], key2_hot[:, par, t, :], key1_hot[:, par, t, :], start=True, stop=True)
                    mm.then_inc(gates_done, 1)

            peeled(pe, BATCHES // 2, gates_pair)
            pe.wait_ge(gates_copied, BATCHES)
            pe.sem_inc(out_done, OUTS)

            def hidden_tile(g, q):
                j = TILE_GROUP * g + q
                pe.wait_ge(ut_loaded[q % 2], 16 * (2 * g + q // 2 + 1))
                pe.wait_ge(hid_gelu, j + 1)
                for c in range(DCH):
                    mm = pe.matmul(bank[:, q % 2, :], ut_ring[:, q % 2, c, :], hT[:, c, DT:SEQ], start=(c == 0), stop=(c == DCH - 1))
                mm.then_inc(hid_done, 1)

            def output_bank(g, par, o, vt_round):
                if o == 0:
                    pe.wait_ge(act_made, TILE_GROUP * (g + 1) + 2)
                    pe.wait_ge(vt_loaded[par], 16 * vt_round)
                pe.wait_ge(out_added, OUTS * g + o + 1)
                for q in range(TILE_GROUP):
                    s = TILE_GROUP * par + q
                    mm = pe.matmul(bank[:, 2 + o % OUT_RING, :], act_ring[:, s, cols(o // 2)], vt_ring[:, s, cols(o % 2, HALF)],
                                   start=(q == 0), stop=(q == TILE_GROUP - 1))
                mm.then_inc(out_done, 1)

            def group(g, par, vt_round):
                for q in range(TILE_GROUP):
                    hidden_tile(g, q)
                    if vt_round is None:
                        continue
                    for o in (2 * q, 2 * q + 1):
                        output_bank(g - 1, 1 - par, o, vt_round)

            group(0, 0, None)
            group(1, 1, 1)
            with pe.Fori(1, TILE_GROUPS // 2) as i:
                group(2 * i, 0, i)
                group(2 * i + 1, 1, i + 1)
            for o in range(OUTS):
                output_bank(TILE_GROUPS - 1, 1, o, TILE_GROUPS // 2)

        @block.vector
        def _(dve):
            def layer_norm(steps, n, src, dst, before_write, release=None, rows=ln_rows):
                dve.bn_stats(stats[:, 0, :], src[:, 0:HALF])
                steps.link(dve.bn_stats(stats[:, 1, :], src[:, HALF:D]))
                dve.bn_aggr(mean_var[:], stats[:]).then_inc(var_ready, 1)
                dve.wait_ge(var_ready, n + 1)
                before_write()
                m = dve.scalar_tensor_tensor(dst, src, mean_var[:, 0:1], rows[:, 0, :], ALU.subtract, ALU.mult)
                if release is not None:
                    m.then_inc(release, 1)
                dve.wait_ge(rstd0_ready, n + 1)
                steps.link(dve.tensor_tensor(newton[:], rstd0[:], rstd0[:], ALU.mult))
                steps.link(dve.scalar_tensor_tensor(newton[:], mean_var[:, 1:2], LN_EPS, newton[:], ALU.add, ALU.mult))
                steps.link(dve.tensor_scalar(newton[:], newton[:], -0.5, 1.5, ALU.mult, ALU.add))
                steps.link(dve.tensor_tensor(rstd[:], rstd0[:], newton[:], ALU.mult))
                return dve.scalar_tensor_tensor(dst, dst, rstd[:], rows[:, 1, :], ALU.mult, ALU.add)

            LN_LINKS = 5
            dve.sem_inc(x_free, 2)
            dve.wait_ge(consts, 1)
            steps = Steps(dve, dve_a, dve_passed)
            steps.link(dve.reciprocal(inv_count[:], inv_count[:]))
            dve.wait_ge(ln_loaded, 32)
            def norm_pair(i):
                steps.at(2 * LN_LINKS * i + 1)
                for par in range(2):
                    n = 2 * i + par
                    dve.wait_ge(x_loaded[par], 16 * (i + 1))

                    def slot_free():
                        need(dve, h0_transposed, 2 * i)
                        need(dve, h0_stored[par], 16 * i)

                    layer_norm(steps, n, xin[:, par, :], normed[:, par, :], slot_free, x_free).then_inc(h0_ready, 1)
                assert steps.k == 2 * LN_LINKS

            peeled(dve, BLOCKS // 2, norm_pair)
            steps = Steps(dve, dve_b)
            dve.wait_ge(small_loaded, 64)
            for g, w in enumerate(POOL_WINDOWS):
                dve.wait_ge(proj_copied, g + 1)
                u = uqk[:, g, :]
                cur, step = u, 1
                spare = [win_a, win_b]
                while step < w:
                    dst = spare.pop(0)
                    dve.tensor_tensor(dst[:, step:], cur[:, step:], cur[:, :SEQ - step], ALU.add)
                    steps.link(dve.tensor_copy(dst[:, :step], cur[:, :step]))
                    if cur is not u:
                        spare.append(cur)
                    cur, step = dst, 2 * step
                steps.link(dve.tensor_tensor(head_cols[:, :w - 1], cur[:, :w - 1], inv_count[:, :w - 1], ALU.mult))
                steps.link(dve.tensor_tensor(head_cols[:, :w - 1], head_cols[:, :w - 1], u[:, :w - 1], ALU.subtract))
                steps.link(dve.scalar_tensor_tensor(u, cur, 1.0 / w, u, ALU.mult, ALU.subtract))
                dve.tensor_copy(u[:, :w - 1], head_cols[:, :w - 1]).then_inc(pooled, 1)
            for g in range(GROUPS):
                dve.wait_ge(pool_mm, g + 1)
                dve.tensor_scalar(uqk[:, g, :], bank[:, 2 * g:2 * g + 2, :].rearrange("p b n -> p (b n)"),
                                  pool_bs[:, 0, g:g + 1], pool_bs[:, 1, g:g + 1], ALU.add, ALU.mult).then_inc(pool_mixed, 1)

            steps = Steps(dve, dve_c, dve_passed)

            def softplus(i, n):
                diagonal = isinstance(i, int) and i == 0
                if diagonal:
                    for c in range(HALVES):
                        zc = z[:, c, :].rearrange("p (h q) -> p h q", q=P)
                        dve.wait_ge(z_done, 2 * n + c + 1)
                        dve.tensor_tensor(zc, zc, cap[:].unsqueeze(1).broadcast_to([P, PER_HALF, P]), ALU.min).then_inc(z_capped, 1)
                for c in range(HALVES):
                    hs = slice(c * PER_HALF, (c + 1) * PER_HALF)
                    zc = z[:, c, :].rearrange("p (h q) -> p h q", q=P)
                    dve.wait_ge(ln_ready, 2 * n + c + 1)
                    need(dve, c_done, 2 * n + c - 1)
                    if not diagonal:
                        dve.wait_ge(sum_ready, 2 * n + c + 1)
                    dve.scalar_tensor_tensor(sp[:, hs], zc, 0.0, soft[:, hs], ALU.max, ALU.add).then_inc(sp_ready, 1)

            def norm_1(b):
                dve.wait_ge(h0_reloaded, 16 * (b + 1))
                dve.wait_ge(y_done, b + 1)
                dve.scalar_tensor_tensor(x1_pre, h0_back, ALPHA, y_ps, ALU.mult, ALU.add).then_inc(y_read, 1)
                dve.wait_ge(y_read, b + 1)

                def slot_free():
                    need(dve, x1_transposed, b)
                    need(dve, x1_stored, 16 * b)

                layer_norm(steps, BLOCKS + b, x1_pre, normed[:, 0, :], slot_free).then_inc(x1_ready, 1)

            softplus(0, 0)
            dve.wait_ge(ln_loaded, 64)
            dve.wait_ge(h0_transposed, BLOCKS)
            dve.wait_ge(h0_stored[0], 16 * (BLOCKS // 2))
            dve.wait_ge(h0_stored[1], 16 * (BLOCKS // 2))
            c_links = LN_LINKS
            with dve.Fori(1, BLOCKS) as b:
                steps.at(c_links * b - LN_LINKS)
                first = first_step(dve, b)
                softplus(0, first)
                norm_1(b - 1)
                assert steps.k == c_links
                with dve.Fori(1, b + 1) as i:
                    softplus(i, dve.snap(first + i))
            steps.at(c_links * BLOCKS - LN_LINKS)
            norm_1(BLOCKS - 1)

            steps = Steps(dve, dve_d, dve_passed)
            dve.sem_inc(score_free, 2)

            def top16(values, work, out_s, out_i, release=None):
                n = len(values)
                for j in range(n):
                    m = dve.max(out_s(j)[:, 0:8], values[j])
                steps.link(m)
                for j in range(n):
                    m = dve.max_index(out_i(j)[:, 0:8], out_s(j)[:, 0:8], values[j])
                for j in range(n):
                    m = dve.match_replace(work(j), out_s(j)[:, 0:8], values[j], LOWEST)
                steps.link(m)
                for j in range(n):
                    m = dve.max(out_s(j)[:, 8:16], work(j))
                steps.link(m)
                for j in range(n):
                    m = dve.max_index(out_i(j)[:, 8:16], out_s(j)[:, 8:16], work(j))
                steps.link(m)

            d_links = 2 * (2 * 4 + 4 + 10)
            with dve.Fori(0, 4) as i:
                steps.at(d_links * i)
                for s in range(4):
                    half = s % 2
                    dve.wait_ge(score_ready, 4 * i + s + 1)
                    dve.sem_inc(dve_passed, 1)
                    score = [bank[:, 4 + 2 * half + b // 4, cols(b % 4)] for b in range(BLOCKS)]
                    top16(score, lambda b: key_work[:, b, :], lambda b: top_s[:, half, b, :], lambda b: top_i[:, half, b, :])
                    dve.tensor_copy(top_if[:, half], top_i[:, half]).then_inc(score_free, 1)
                    if not half:
                        continue
                    h = 2 * i + s // 2
                    dve.wait_ge(score_free, 4 * i + s + 3)
                    steps.link(dve.tensor_scalar(top_if[:, 0], top_if[:, 0], float(N_KEYS), None, ALU.mult))
                    for lists, dst in ((top_s, cand), (top_if, cand_e)):
                        for a in range(5):
                            n = ROW_LEN[a]
                            m = dve.tensor_tensor(dst[:, :, ROW_AT[a]:ROW_AT[a] + n], lists[:, 1, :, 0:n],
                                                  lists[:, 0, :, a:a + 1].broadcast_to([P, BLOCKS, n]), ALU.add)
                        m = dve.tensor_tensor(dst[:, :, ROW_AT[5]:ROW_AT[8]].rearrange("p b (a n) -> p b a n", n=2),
                                              lists[:, 1, :, 0:2].unsqueeze(2).broadcast_to([P, BLOCKS, 3, 2]),
                                              lists[:, 0, :, 5:8].unsqueeze(3).broadcast_to([P, BLOCKS, 3, 2]), ALU.add)
                        m = dve.tensor_tensor(dst[:, :, ROW_AT[8]:CANDS], lists[:, 0, :, 8:16],
                                              lists[:, 1, :, 0:1].broadcast_to([P, BLOCKS, 8]), ALU.add)
                    steps.link(m)
                    top16([cand[:, b, :] for b in range(BLOCKS)], lambda b: cand_w[:, b, :],
                          lambda b: best_s[:, b, :], lambda b: best_p[:, b, :])
                    steps.link(dve.tensor_copy(best_pf, best_p))
                    flat_p = best_pf.rearrange("p b k -> p (b k)")
                    steps.link(dve.tensor_tensor(match, iota_k[:, 0:CANDS].unsqueeze(1).broadcast_to([P, BLOCKS * TOPK, CANDS]),
                                                 flat_p.unsqueeze(2).broadcast_to([P, BLOCKS * TOPK, CANDS]), ALU.is_equal))
                    match4 = match.rearrange("p (b k) c -> p b k c", k=TOPK)
                    steps.link(dve.tensor_tensor(match4, match4, cand_e.unsqueeze(2).broadcast_to([P, BLOCKS, TOPK, CANDS]), ALU.mult))
                    steps.link(dve.tensor_reduce(flat_p, match, AX.X, ALU.add))
                    idx_h = idx_all[:, 0:UNITS * TOPK].rearrange("p (b m) -> p b m", b=BLOCKS)[:, :, cols(h, TOPK)]
                    gate_h = gate_all.rearrange("p (b m) -> p b m", b=BLOCKS)[:, :, cols(h, TOPK)]
                    dve.tensor_copy(idx_h, best_pf)
                    steps.link(dve.tensor_copy(gate_sum[:], best_s[:, :, 0]))
                    dve.tensor_tensor(best_s, best_s, gate_sum[:].unsqueeze(2).broadcast_to([P, BLOCKS, TOPK]), ALU.subtract).then_inc(gate_in, 1)
                    dve.wait_ge(gate_exp, h + 1)
                    steps.link(dve.tensor_reduce(gate_sum[:], best_s, AX.X, ALU.add))
                    steps.link(dve.reciprocal(gate_sum[:], gate_sum[:]))
                    steps.link(dve.tensor_tensor(gate_h, best_s, gate_sum[:].unsqueeze(2).broadcast_to([P, BLOCKS, TOPK]), ALU.mult))
                assert steps.k == d_links, steps.k
            steps.at(4 * d_links)
            dve.wait_ge(res_init, BLOCKS)
            later = idx_all[:, GATHERED * PICKS:BLOCKS * PICKS]
            steps.link(dve.tensor_scalar(pick_cols[:, 0, :].bitcast(U32), later, 7, None, ALU.logical_shift_right))
            steps.link(dve.tensor_scalar(pick_cols[:, 1, :].bitcast(U32), later, N_KEYS - 1, None, ALU.bitwise_and))
            for r in range(2):
                steps.link(dve.tensor_copy(pick_cols[:, r, :], pick_cols[:, r, :].bitcast(U32)))
            dve.tensor_copy(pick_cols[:, 2, :], gate_all[:, GATHERED * PICKS:BLOCKS * PICKS]).then_inc(picks_split, 1)
            dve.wait_ge(picks_kept, 3)
            def hot_batch(t, par):
                for r, hot, ready in ((0, key1_hot, key1_ready), (1, key2_hot, key2_ready)):
                    dve.tensor_tensor(hot[:, par], iota_k[:].unsqueeze(1).broadcast_to([P, BATCH, N_KEYS]),
                                      pick_rows[:, r, bass.ds(t * BATCH, BATCH)].unsqueeze(2).broadcast_to([P, BATCH, N_KEYS]),
                                      ALU.is_equal).then_inc(ready, 1)

            hot_batch(0, 0)
            hot_batch(1, 1)
            with dve.Fori(1, BATCHES // 2) as i:
                for par in range(2):
                    dve.wait_ge(gates_done, 2 * i + par - 1)
                    hot_batch(2 * i + par, par)
            dve.sem_inc(u_free, U_RING)
            dve.sem_inc(v_free, V_RING)
            dve.sem_inc(act_ready, 2)
            dve.sem_inc(act_made, 2)
            dve.sem_inc(out_added, OUT_RING)
            dve.wait_ge(x1_back, 16)
            dve.wait_ge(gates_done, BATCHES)
            dve.tensor_copy(idx_u[:, 0, :], idx_all[:, 0:TOPK]).then_inc(idx_u_staged, 1)

            def of_block(tokens, b):
                return tokens[:, bass.ds(b, 1), :].rearrange("p o d -> p (o d)")

            def weigh(n, par):
                dve.wait_ge(gelu_done, n + 1)
                dve.tensor_tensor(act_g[:, par, :], hid_g[:, par, :], gate_all[:, cols(n, TOPK)], ALU.mult).then_inc(act_ready, 1)
                dve.wait_ge(act_ready, n + 3)

            def dot(n, par, k, b):
                s = k % U_RING
                dve.wait_ge(u_loaded[s], 16 * (TOPK // U_RING * n + k // U_RING + 1))
                row = u_ring[:, s, :]
                dve.scalar_tensor_tensor(row, row, 1.0, of_block(x1_all, b), ALU.mult, ALU.mult,
                                         accum_out=hid[:, par, k:k + 1]).then_inc(u_free, 1)

            def add_row(n, par, k, b):
                s = k % V_RING
                dve.wait_ge(v_loaded[s], 16 * (TOPK // V_RING * n + k // V_RING + 1))
                dve.wait_ge(v_free, V_RING + TOPK * n + k)
                dve.scalar_tensor_tensor(of_block(res, b), v_ring[:, s, :], act_g[:, par, k:k + 1], of_block(res, b),
                                         ALU.mult, ALU.add).then_inc(v_free, 1)

            def gate_tile(g, par, q):
                dve.wait_ge(hid_gelu, TILE_GROUP * g + q + 3)
                dve.wait_ge(gt_loaded[q], 16 * (g + 1))
                if q == 0:
                    need(dve, out_done, OUTS * g)
                dve.tensor_tensor(act_ring[:, TILE_GROUP * par + q, :], gelu_ring[:, q % 2, :], g_ring[:, q, :], ALU.mult).then_inc(act_made, 1)

            def add_output(g, o):
                dve.wait_ge(out_done, OUTS * (g + 1) + o + 1)
                r = res[:, GATHERED + o // 2, cols(o % 2, HALF)]
                dve.tensor_tensor(r, r, bank[:, 2 + o % OUT_RING, :], ALU.add).then_inc(out_added, 1)

            def unit(n, par, b, b_before, first=False):
                if not first:
                    dve.wait_ge(out_added, OUTS * (n - 1) + OUT_RING)
                for k in range(TOPK):
                    dot(n, par, k, b)
                    if k == 1 and not first:
                        weigh(n - 1, 1 - par)
                    if k >= 1 and not first:
                        add_row(n - 1, 1 - par, k - 1, b_before)
                    if k == 3:
                        dve.tensor_copy(idx_v[:, par, :], idx_all[:, cols(n, TOPK)]).then_inc(idx_v_staged, 1)
                        dve.tensor_copy(idx_u[:, 1 - par, :], idx_all[:, cols(n + 1, TOPK)]).then_inc(idx_u_staged, 1)
                    if k % 4 == 3:
                        gate_tile(n, par, k // 4)
                        if not first:
                            for o in (k // 4 * 2, k // 4 * 2 + 1):
                                add_output(n - 1, o)
                if not first:
                    add_row(n - 1, 1 - par, TOPK - 1, b_before)

            unit(0, 0, 0, 0, True)
            unit(1, 1, 0, 0)
            with dve.Fori(1, G_UNITS // 2) as i:
                blk = dve.snap(i // 4)
                unit(2 * i, 0, blk, dve.snap((2 * i - 1) // 8))
                unit(2 * i + 1, 1, blk, blk)
            weigh(G_UNITS - 1, 1)
            dve.wait_ge(out_added, OUTS * (TILE_GROUPS - 1) + OUT_RING)
            for k in range(TOPK):
                add_row(G_UNITS - 1, 1, k, GATHERED - 1)
                if k % 2:
                    add_output(TILE_GROUPS - 1, k // 2)
            dve.wait_ge(v_free, V_RING + TOPK * G_UNITS)
            dve.wait_ge(out_added, OUTS * TILE_GROUPS + OUT_RING)
            dve.wait_ge(ln_loaded, 96)
            steps = Steps(dve, dve_e, dve_passed)
            def norm_out_pair(i):
                steps.at(2 * LN_LINKS * i)
                for par in range(2):
                    n = 2 * i + par

                    def slot_free():
                        need(dve, out_stored[par], 16 * i)

                    layer_norm(steps, 2 * BLOCKS + n, res[:, bass.ds(n, 1), :].rearrange("p o d -> p (o d)"),
                               normed[:, par, :], slot_free, rows=ln2_rows).then_inc(out_ready, 1)

            peeled(dve, BLOCKS // 2, norm_out_pair)


def kernel(**inputs):
    import numpy as _np
    import concourse.bacc as _bacc
    from concourse import mybir as _mybir
    from concourse.bass_utils import run_bass_kernel_spmd as _run

    a = {k: _np.asarray(v) for k, v in inputs.items()}
    w_in = a["w_in"][0]
    laid = {
        "x": a["x"].reshape(SEQ, D),
        "ln0_g": a["ln0_g"], "ln0_b": a["ln0_b"],
        "w_in_chunks": w_in[:, :12 * P].reshape(DCH, P, 12, P).transpose(2, 1, 0, 3),
        "w_v": w_in[:, 12 * P:],
        "pool_w": a["pool_w"][0],
        "pool_b": a["pool_b"][0].T,
        "pool_scale": a["pool_scale"][0].reshape(GROUPS, P).T,
        "w_out": a["w_out"][0],
        "ln1_g": a["ln1_g"][0], "ln1_b": a["ln1_b"][0],
        "wq_chunks": a["peer_wq"][0].reshape(DCH, P, 16, P).transpose(2, 1, 0, 3),
        "keys_t": a["peer_sub_keys"][0].transpose(0, 2, 1),
        "peer_u": a["peer_u"][0], "peer_v": a["peer_v"][0],
        "u_tiles": a["peer_u"][0].reshape(TILES, P, DCH, P).transpose(0, 3, 2, 1),
        "ln2_g": a["ln2_g"][0], "ln2_b": a["ln2_b"][0],
    }
    nc = _bacc.Bacc("TRN2", target_bir_lowering=False, num_devices=1)
    arrays, args = {}, []
    for name, v in laid.items():
        v = _np.ascontiguousarray(v)
        arrays[f"in_{name}"] = v
        args.append(nc.dram_tensor(f"in_{name}", v.shape, _mybir.dt.from_np(v.dtype), kind="ExternalInput").ap())
    o = nc.dram_tensor("out_0", (SEQ, D), F32, kind="ExternalOutput").ap()
    layer_kernel(nc, *args, o)
    r = _run(nc, [arrays], core_ids=[0])
    return r.results[0]["out_0"].reshape(a["x"].shape)
```

```python
import math
from contextlib import ExitStack

import concourse.bass as bass
from concourse import mybir

F32 = mybir.dt.float32
BF16 = mybir.dt.bfloat16
U32 = mybir.dt.uint32
ALU = mybir.AluOpType
ACT = mybir.ActivationFunctionType
AX = mybir.AxisListType

P = 128
SEQ = 1024
D = 1024
BLOCKS = SEQ // P
DCH = D // P
HALF = 512
POOL_WINDOWS = (2, 4, 8, 16)
GROUPS = len(POOL_WINDOWS)
HEADS = 8
HEAD_DIM = 64
HALVES = 2
PER_HALF = HEADS // HALVES
PEER_HEADS = 8
N_KEYS = 128
TOPK = 16
PICKS = PEER_HEADS * TOPK
UNITS = BLOCKS * PEER_HEADS
GATHERED = BLOCKS // 2
G_UNITS = GATHERED * PEER_HEADS
DENSE = BLOCKS - GATHERED
DT = DENSE * P
TILES = N_KEYS
TILE_GROUP = 4
TILE_GROUPS = TILES // TILE_GROUP
assert TILE_GROUPS == G_UNITS and DT == 512
OUTS = 2 * DENSE
OUT_RING = 4
BATCH = 8
HOT_RING = 4
BATCHES = DT // BATCH
BLOCK_BATCHES = P // BATCH
KEY_HALF = N_KEYS // 2
LN_EPS = 1e-5
ALPHA = 2.0 ** 0.25
CAP_OPEN = 3.0e38
CAP_SHUT = -1.0e30
LOWEST = -3.0e38
U_RING = 4
V_RING = 8
ROW_LEN = [TOPK // (a + 1) for a in range(TOPK)]
ROW_AT = [sum(ROW_LEN[:a]) for a in range(TOPK)]
CANDS = sum(ROW_LEN)
FOLDED = (CANDS // 2 + 1) // 2
assert CANDS % 2 == 0


def need(engine, semaphore, value):
    if isinstance(value, int) and value <= 0:
        return
    engine.wait_ge(semaphore, value)


def peeled(engine, count, body):
    body(0)
    with engine.Fori(1, count) as i:
        body(i)


class Steps:

    def __init__(self, engine, semaphore, passed=None):
        self.engine, self.semaphore, self.passed, self.base, self.k = engine, semaphore, passed, 0, 0

    def at(self, base):
        self.base, self.k = base, 0

    def link(self, instruction):
        self.k += 1
        instruction.then_inc(self.semaphore, 1)
        self.engine.wait_ge(self.semaphore, self.base + self.k)
        if self.passed is not None:
            self.engine.sem_inc(self.passed, 1)


def layer_kernel(nc, x, ln0_g, ln0_b, w_in_chunks, w_v, pool_w, pool_b, pool_scale, w_out,
                 ln1_g, ln1_b, wq_chunks, keys_t, peer_u, peer_v, u_tiles, ln2_g, ln2_b, out):
    x_blocks = x.rearrange("(b p) d -> b p d", p=P)
    out_blocks = out.rearrange("(b p) d -> b p d", p=P)
    h0_dram = nc.dram_tensor("h0_scratch", (BLOCKS, P, D), F32).ap()
    g_dram = nc.dram_tensor("gates_scratch", (TILES, P, DT), F32).ap()
    v_tiles = peer_v.rearrange("(j e) d -> j e d", e=P)
    x1_dram = nc.dram_tensor("x1_scratch", (BLOCKS, P, D), F32).ap()

    ctx = ExitStack()
    with ctx:
        def sb(name, shape, dt=F32):
            return ctx.enter_context(nc.sbuf_tensor(name, shape, dt))

        def sem(name):
            return ctx.enter_context(nc.semaphore(name))

        KIB = 256
        arena = sb("arena", [P, 196 * KIB])

        def region(kib, cols):
            return arena[:, int(kib * KIB):int(kib * KIB) + cols]

        hT = region(0, DCH * SEQ).rearrange("p (c t) -> p c t", c=DCH)
        act_ring = hT[:, :, 0:DT]
        uqk = region(32, 12 * SEQ).rearrange("p (m t) -> p m t", m=12)
        x1_all = region(32, BLOCKS * D).rearrange("p (b d) -> p b d", b=BLOCKS)
        wo = region(80, DCH * D).rearrange("p (c d) -> p c d", c=DCH)
        wv = region(80, DCH * HALF).rearrange("p (c d) -> p c d", c=DCH)
        res = region(80, BLOCKS * D).rearrange("p (b d) -> p b d", b=BLOCKS)
        v_all = region(112, BLOCKS * HALF).rearrange("p (b d) -> p b d", b=BLOCKS)
        w_ring = region(128, 4 * D).rearrange("p (s c n) -> p s c n", s=4, c=DCH)
        pick_cols = region(48, 3 * DT).rearrange("p (r t) -> p r t", r=3)
        pick_rows = region(72.5, 3 * DT).rearrange("p (r t) -> p r t", r=3)
        key1_hot = hT[:, :, 0:DT].rearrange("p (s c) (t n) -> p s c t n", s=HOT_RING, n=N_KEYS)
        key2_hot = region(176, HOT_RING * BATCH * P).rearrange("p (s c t n) -> p s c t n", s=HOT_RING, c=BATCH // 4, t=4)
        gates = [[region(kib, KEY_HALF * P).rearrange("p (n t) -> p n t", n=KEY_HALF) for kib in slot]
                 for slot in ((32, 80), (112, 144))]
        u_ring = region(48, U_RING * D).rearrange("p (s d) -> p s d", s=U_RING)
        v_ring = region(112, V_RING * D).rearrange("p (s d) -> p s d", s=V_RING)
        ut_ring = region(144, 2 * D).rearrange("p (s c e) -> p s c e", s=2, c=DCH)
        vt_ring = region(152, 8 * D).rearrange("p (s d) -> p s d", s=8)
        g_ring = region(184, 4 * DT).rearrange("p (s t) -> p s t", s=4)
        gelu_ring = region(192, 2 * DT).rearrange("p (s t) -> p s t", s=2)
        ln2_rows = region(72, 2 * D).rearrange("p (r d) -> p r d", r=2)
        ln_rows = region(144, 2 * D).rearrange("p (r d) -> p r d", r=2)
        xin = region(152, 2 * D).rearrange("p (s d) -> p s d", s=2)
        qpeer = region(152, 2 * D).rearrange("p (s d) -> p s d", s=2)
        normed = region(160, 2 * D).rearrange("p (s d) -> p s d", s=2)
        h0_back = region(152, D)
        x1_pre = region(156, D)
        q_pad = region(168, HEADS * P).rearrange("p (h q) -> p h q", h=HEADS)
        sp = region(172, HEADS * P).rearrange("p (h q) -> p h q", h=HEADS)
        sp_sum = region(176, HEADS * P).rearrange("p (h q) -> p h q", h=HEADS)
        attn = region(180, HEADS * P).rearrange("p (h q) -> p h q", h=HEADS)
        soft = region(184, HEADS * P).rearrange("p (h q) -> p h q", h=HEADS)
        mix_t = region(188, DCH * P).rearrange("p (c q) -> p c q", c=DCH)
        k_stage = region(192, 4 * P).rearrange("p (c k) -> p c k", c=4)
        o_stage = region(194, HALF)
        win_a = region(172, SEQ)
        win_b = region(176, SEQ)
        match = [region(kib, BLOCKS * TOPK * CANDS).rearrange("p (g c) -> p g c", c=CANDS) for kib in (168, 80)]
        idx_all = region(64, UNITS * TOPK + TOPK).bitcast(U32)
        gate_all = region(68.25, UNITS * TOPK)
        key_work = region(72.5, BLOCKS * N_KEYS).rearrange("p (b n) -> p b n", b=BLOCKS)

        def small(name, shape, dt=F32):
            return sb(name, shape, dt)

        ident = small("ident", [P, P])
        neg_tri = small("neg_tri", [P, P])
        neg_ones = small("neg_ones", [P, P])
        cap = small("cap", [P, P])
        keys_sb = small("keys_sb", [P, 2, N_KEYS])
        pool_w_sb = small("pool_w_sb", [P, GROUPS, P])
        pool_bs = small("pool_bs", [P, 2, GROUPS])
        kind_scale = small("kind_scale", [P, 3])
        inv_count = small("inv_count", [P, TOPK])
        head_cols = small("head_cols", [P, TOPK])
        iota_k = small("iota_k", [P, N_KEYS])
        stats = small("stats", [P, 2, 2, 6])
        mean_var = small("mean_var", [P, 2, 2])
        eps_col = small("eps_col", [P, 1])
        one_col = small("one_col", [P, 1])
        zero_row = small("zero_row", [1, P])
        lnv = small("lnv", [P, 2])
        rstd0 = small("rstd0", [P, 2])
        newton = small("newton", [P, 1])
        rstd = small("rstd", [P, 1])
        top_s = region(112, 2 * BLOCKS * TOPK).rearrange("p (h b k) -> p h b k", h=2, b=BLOCKS)
        top_i = region(113, 2 * BLOCKS * TOPK).bitcast(U32).rearrange("p (h b k) -> p h b k", h=2, b=BLOCKS)
        top_if = region(114, 2 * BLOCKS * TOPK).rearrange("p (h b k) -> p h b k", h=2, b=BLOCKS)
        cand = region(115, BLOCKS * CANDS).rearrange("p (b k) -> p b k", b=BLOCKS)
        cand_e = [region(kib, BLOCKS * CANDS).rearrange("p (b k) -> p b k", b=BLOCKS) for kib in (105, 107)]
        cand_w = region(118.5, BLOCKS * CANDS).rearrange("p (b k) -> p b k", b=BLOCKS)
        best_s = [region(kib, BLOCKS * TOPK).rearrange("p (b k) -> p b k", b=BLOCKS) for kib in (120.25, 109)]
        expert_f = region(110, BLOCKS * TOPK)
        best_p = region(120.75, BLOCKS * TOPK).bitcast(U32).rearrange("p (b k) -> p b k", b=BLOCKS)
        best_pf = region(121.25, BLOCKS * TOPK).rearrange("p (b k) -> p b k", b=BLOCKS)
        gate_sum = small("gate_sum", [P, BLOCKS])
        idx_u = small("idx_u", [P, 2, TOPK], U32)
        idx_v = small("idx_v", [P, 2, TOPK], U32)
        hid = small("hid", [P, 2, TOPK])
        hid_g = small("hid_g", [P, 2, TOPK])
        act_g = small("act_g", [P, 2, TOPK])

        bank = ctx.enter_context(nc.psum_tensor("bank", [P, 8, HALF], F32))
        z = bank[:, 0:2, :]
        o_ps = bank[:, 2, :]
        oT_ps = bank[:, 3, :].rearrange("p (c q) -> p c q", c=4)
        y_ps = bank[:, 4:6, :].rearrange("p b n -> p (b n)")
        xT_ps = bank[:, 6:8, :].rearrange("p b (c q) -> p (b c) q", q=P)

        consts = sem("consts_made")
        const_step = sem("const_step")
        ln_loaded = sem("ln_loaded")
        small_loaded = sem("small_weights_loaded")
        x_loaded = [sem(f"x_loaded{i}") for i in range(2)]
        x_free = sem("x_slot_free")
        h0_ready = sem("h0_ready")
        h0_stored = [sem(f"h0_stored{i}") for i in range(2)]
        h0_transposed = sem("h0_transposed")
        h0t_copied = sem("h0t_copied")
        w_loaded = [sem(f"w_loaded{i}") for i in range(4)]
        wv_loaded = sem("wv_loaded")
        wo_loaded = sem("wo_loaded")
        proj_done = sem("proj_done")
        proj_copied = sem("proj_copied")
        v_done = sem("v_done")
        v_copied = sem("v_copied")
        pooled = sem("pooled")
        pool_mm = sem("pool_mm_done")
        pool_mixed = sem("pool_mixed")
        var_ready = sem("var_ready")
        rstd0_ready = sem("rstd0_ready")
        act_step = sem("act_step")
        pool_passed = sem("pool_passed_wait")
        dve_passed = sem("dve_passed_wait")
        dve_a = sem("dve_step_a")
        dve_b = sem("dve_step_b")
        dve_c = sem("dve_step_c")
        dve_d = sem("dve_step_d")
        dve_e = sem("dve_step_e")
        q_staged = sem("q_staged")
        k_staged = sem("k_staged")
        z_done = sem("z_done")
        z_capped = sem("z_capped")
        ln_ready = sem("ln_ready")
        sp_ready = sem("sp_ready")
        sum_ready = sem("sum_ready")
        c_done = sem("c_done")
        a_ready = sem("a_ready")
        av_done = sem("av_done")
        o_copied = sem("o_copied")
        o_transposed = sem("o_transposed")
        mix_copied = sem("mix_copied")
        mixp_staged = sem("mixp_staged")
        y_done = sem("y_done")
        y_read = sem("y_read")
        h0_reloaded = sem("h0_reloaded")
        x1_ready = sem("x1_ready")
        x1_transposed = sem("x1_transposed")
        x1t_copied = sem("x1t_copied")
        x1_stored = sem("x1_stored")
        wq_done = sem("wq_done")
        qp_copied = sem("qp_copied")
        score_ready = sem("score_ready")
        score_free = sem("score_bank_free")
        gate_in = sem("gate_in_ready")
        gate_exp = sem("gate_exp_ready")
        x1_back = sem("x1_back")
        res_init = sem("residual_scaled")
        picks_split = sem("picks_split")
        picks_turned = sem("picks_turned")
        picks_kept = sem("picks_kept")
        key1_gated = sem("key1_hot_gated")
        key1_ready = sem("key1_hot_ready")
        key2_ready = sem("key2_hot_ready")
        gates_done = sem("gates_done")
        gates_copied = sem("gates_copied")
        gates_stored = [sem(f"gates_stored{i}") for i in range(2)]
        match_ready = sem("match_ready")
        match_weighed = sem("match_weighed")
        match_folded = sem("match_folded")
        ut_loaded = [sem(f"u_tile_loaded{i}") for i in range(2)]
        vt_loaded = [sem(f"v_tile_loaded{i}") for i in range(2)]
        gt_loaded = [sem(f"gate_tile_loaded{i}") for i in range(4)]
        hid_done = sem("hidden_tile_done")
        hid_gelu = sem("hidden_tile_gelu")
        act_made = sem("act_tile_made")
        out_done = sem("out_bank_done")
        out_added = sem("out_bank_added")
        idx_u_staged = sem("idx_u_staged")
        idx_v_staged = sem("idx_v_staged")
        u_loaded = [sem(f"u_loaded{i}") for i in range(U_RING)]
        v_loaded = [sem(f"v_loaded{i}") for i in range(V_RING)]
        u_free = sem("u_slot_free")
        v_free = sem("v_slot_free")
        gelu_done = sem("gelu_done")
        act_ready = sem("act_ready")
        out_ready = sem("out_ready")
        out_stored = sem("out_stored")

        block = ctx.enter_context(nc.Block())

        def block_of(ap, n):
            return ap[bass.ds(n, 1)].rearrange("o p d -> p (o d)")

        def cols(n, width=P):
            return bass.ds(n * width, width)

        def pairs_before(b):
            return b * (b + 1) // 2

        def first_step(engine, b):
            return engine.snap(engine.snap((b - 1) * (b + 2) // 2) + 1)

        def key_block(b, i):
            if isinstance(b, int):
                return b - i
            return nc.s_assert_within(b - i, 0, BLOCKS - 1, skip_runtime_bounds_check_because="i runs from 0 to b")

        def per_token(r, t):
            return pick_rows[:, r, bass.ds(t * BATCH, BATCH)].rearrange("p (c t) -> p c t", t=4).unsqueeze(3).broadcast_to([P, BATCH // 4, 4, N_KEYS])

        @block.sync
        def _(sync):
            def load_ln(g, b, rows=ln_rows):
                sync.dma_start(rows[:, 0, :], g.partition_broadcast(P)).then_inc(ln_loaded, 16)
                sync.dma_start(rows[:, 1, :], b.partition_broadcast(P)).then_inc(ln_loaded, 16)

            def load_x(n, par):
                sync.dma_start(xin[:, par, :], block_of(x_blocks, n)).then_inc(x_loaded[par], 16)

            load_x(0, 0)
            load_ln(ln0_g, ln0_b)
            load_x(1, 1)
            with sync.Fori(1, BLOCKS // 2) as i:
                for par in range(2):
                    n = 2 * i + par
                    sync.wait_ge(x_free, n - 1)
                    load_x(n, par)
            with sync.Fori(1, 3) as kind:
                for s in range(4):
                    sync.wait_ge(proj_done, 4 * kind + s - 3)
                    sync.dma_start(w_ring[:, s], w_in_chunks[bass.ds(4 * kind + s, 1)].rearrange("o p c n -> p (o c) n")).then_inc(w_loaded[s], 16)
            sync.wait_ge(h0_ready, BLOCKS)
            load_ln(ln1_g, ln1_b)
            for s in range(4):
                sync.wait_ge(proj_done, 9 + s)
                sync.dma_start(w_ring[:, s], wq_chunks[s]).then_inc(w_loaded[s], 16)
            sync.wait_ge(v_done, BLOCKS)
            sync.dma_start(wo, w_out.rearrange("(c p) d -> p c d", p=P)).then_inc(wo_loaded, 16)
            for par in range(2):
                sync.wait_ge(h0_stored[par], 16 * (BLOCKS // 2))
            def stage_c_block(b):
                need(sync, y_read, b)
                sync.dma_start(h0_back, block_of(h0_dram, b)).then_inc(h0_reloaded, 16)
                sync.wait_ge(x1_ready, b + 1)
                sync.dma_start(block_of(x1_dram, b), normed[:, 0, :]).then_inc(x1_stored, 16)

            peeled(sync, BLOCKS, stage_c_block)
            with sync.Fori(1, 4) as i:
                for s in range(4):
                    sync.wait_ge(wq_done, 4 * i + s - 3)
                    sync.dma_start(w_ring[:, s], wq_chunks[bass.ds(4 * i + s, 1)].rearrange("o p c n -> p (o c) n")).then_inc(w_loaded[s], 16)
            for b in range(DENSE):
                sync.wait_ge(gates_copied, BLOCK_BATCHES * (b + 1))
                for kh in range(2):
                    sync.dma_start(g_dram[kh * KEY_HALF:(kh + 1) * KEY_HALF, :, cols(b)].rearrange("n p t -> p n t"),
                                   gates[b % 2][kh]).then_inc(gates_stored[b % 2], 16)
                if b == DENSE - 2:
                    sync.wait_ge(gates_stored[0], 16 * DENSE)
                    sync.wait_ge(x1_stored, 16 * BLOCKS)
                    sync.dma_start(x1_all, x1_dram.rearrange("b p d -> p b d")).then_inc(x1_back, 16)
            for par in range(2):
                sync.wait_ge(gates_stored[par], 16 * DENSE)
            load_ln(ln2_g, ln2_b, ln2_rows)

            def load_v_group(g, par):
                tiles = v_tiles[0:TILE_GROUP] if isinstance(g, int) and g == 0 else v_tiles[bass.ds(g * TILE_GROUP, TILE_GROUP)]
                sync.dma_start(vt_ring[:, TILE_GROUP * par:TILE_GROUP * (par + 1), :], tiles.rearrange("j e d -> e j d")).then_inc(vt_loaded[par], 16)

            load_v_group(0, 0)
            load_v_group(1, 1)
            with sync.Fori(1, TILE_GROUPS // 2) as i:
                for par in range(2):
                    g = 2 * i + par
                    sync.wait_ge(out_done, OUTS * g)
                    load_v_group(g, par)
            with sync.Fori(0, BLOCKS) as b:
                sync.wait_ge(out_ready, b + 1)
                sync.dma_start(block_of(out_blocks, b), res[:, bass.ds(b, 1), :].rearrange("p o d -> p (o d)")).then_inc(out_stored, 16)
            sync.wait_ge(out_stored, 16 * BLOCKS)

        @block.gpsimd
        def _(pool):
            pool.memset(ident[:], 0.0)
            pool.memset(neg_tri[:], -1.0)
            pool.memset(neg_ones[:], -1.0)
            pool.memset(cap[:], CAP_OPEN)
            pool.memset(kind_scale[:], 1.0)
            pool.memset(eps_col[:], LN_EPS)
            pool.memset(one_col[:], 1.0)
            pool.memset(zero_row[:], 0.0)
            pool.memset(q_pad, 0.0)
            pool.memset(idx_u[:], 0)
            pool.iota(iota_k[:], pattern=[[1, N_KEYS]], base=0, channel_multiplier=0, allow_small_or_imprecise_dtypes=True)
            pool.iota(inv_count[:], pattern=[[1, TOPK]], base=1, channel_multiplier=0, allow_small_or_imprecise_dtypes=True).then_inc(const_step, 1)
            pool.wait_ge(const_step, 1)
            pool.affine_select(out=ident[:], in_=ident[:], compare_op=ALU.not_equal, fill=1.0, base=0,
                               pattern=[[-1, P]], channel_multiplier=1)
            pool.affine_select(out=neg_tri[:], in_=neg_tri[:], compare_op=ALU.is_ge, fill=0.0, base=0,
                               pattern=[[-1, P]], channel_multiplier=1)
            pool.affine_select(out=cap[:], in_=cap[:], compare_op=ALU.is_gt, fill=CAP_SHUT, base=0,
                               pattern=[[1, P]], channel_multiplier=-1)
            pool.memset(kind_scale[:, 1:2], HEAD_DIM ** -0.5).then_inc(consts, 1)
            with pool.Fori(0, BLOCKS // 2) as i:
                for par in range(2):
                    n = 2 * i + par
                    pool.wait_ge(h0_ready, n + 1)
                    pool.dma_start(block_of(h0_dram, n), normed[:, par, :]).then_inc(h0_stored[par], 16)

            def begin_block(b, n):
                need(pool, z_done, 2 * n)
                pool.tensor_copy(k_stage, uqk[:, 8:12, cols(b)]).then_inc(k_staged, 1)
                need(pool, c_done, 2 * n)
                pool.sem_inc(pool_passed, 1)
                for c in range(HALVES):
                    pool.memset(sp_sum[:, c * PER_HALF:(c + 1) * PER_HALF], 0.0).then_inc(sum_ready, 1)

            def later_keys(b, i, n):
                pool.wait_ge(z_done, 2 * n)
                pool.tensor_copy(k_stage, uqk[:, 8:12, cols(key_block(b, i))]).then_inc(k_staged, 1)
                for c in range(HALVES):
                    hs = slice(c * PER_HALF, (c + 1) * PER_HALF)
                    pool.wait_ge(sum_ready, 2 * n + c - 1)
                    pool.wait_ge(sp_ready, 2 * n + c - 1)
                    pool.wait_ge(c_done, 2 * n + c - 1)
                    pool.tensor_tensor(sp_sum[:, hs], sp_sum[:, hs], sp[:, hs], ALU.add).then_inc(sum_ready, 1)

            pool.wait_ge(proj_copied, 12)
            pool.wait_ge(pool_mixed, GROUPS)
            begin_block(0, 0)
            with pool.Fori(1, BLOCKS) as b:
                first = first_step(pool, b)
                begin_block(b, first)
                with pool.Fori(1, b + 1) as i:
                    later_keys(b, i, pool.snap(first + i))

            with pool.Fori(0, PEER_HEADS // 2) as i:
                for par in range(2):
                    pool.wait_ge(match_ready, 2 * i + par + 1)
                    match4 = match[par].rearrange("p (b k) c -> p b k c", k=TOPK)
                    pool.tensor_tensor(match4, match4, cand_e[par].unsqueeze(2).broadcast_to([P, BLOCKS, TOPK, CANDS]),
                                       ALU.mult).then_inc(match_folded, 1)
                    pool.wait_ge(match_folded, 2 * (2 * i + par) + 1)
                    pool.tensor_tensor(match[par][:, :, 0:CANDS // 2], match[par][:, :, 0:CANDS // 2], match[par][:, :, CANDS // 2:CANDS],
                                       ALU.add).then_inc(match_folded, 1)
                    pool.wait_ge(match_folded, 2 * (2 * i + par) + 2)
                    rest = CANDS // 2 - FOLDED
                    pool.tensor_tensor(match[par][:, :, 0:rest], match[par][:, :, 0:rest], match[par][:, :, FOLDED:CANDS // 2],
                                       ALU.add).then_inc(match_weighed, 1)

            def gate_batch(t, par):
                pool.wait_ge(key1_ready, t + 1)
                pool.tensor_tensor(key1_hot[:, par], key1_hot[:, par], per_token(2, t),
                                   ALU.mult).then_inc(key1_gated, 1)

            with pool.Fori(0, BATCHES // HOT_RING) as i:
                for slot in range(HOT_RING):
                    gate_batch(HOT_RING * i + slot, slot)

            for par in range(2):
                pool.wait_ge(gates_stored[par], 16 * DENSE)
            pool.wait_ge(res_init, BLOCKS)

            def gathers(u_unit, u_par, v_unit, v_par):
                if u_unit is not None:
                    pool.wait_ge(idx_u_staged, u_unit + 1)
                if v_unit is not None:
                    pool.wait_ge(idx_v_staged, v_unit + 1)
                for k in range(TOPK):
                    if u_unit is not None:
                        pool.wait_ge(u_free, TOPK * u_unit + k + 1)
                        pool.sem_inc(pool_passed, 1)
                        pool.indirect_dma_start(u_ring[:, k % U_RING, :], None, peer_u,
                                                bass.IndirectOffsetOnAxis(ap=idx_u[:, u_par, k:k + 1], axis=0)).then_inc(u_loaded[k % U_RING], 16)
                    if v_unit is not None:
                        pool.wait_ge(v_free, TOPK * v_unit + k + 1)
                        pool.sem_inc(pool_passed, 1)
                        pool.indirect_dma_start(v_ring[:, k % V_RING, :], None, peer_v,
                                                bass.IndirectOffsetOnAxis(ap=idx_v[:, v_par, k:k + 1], axis=0)).then_inc(v_loaded[k % V_RING], 16)

            gathers(0, 0, None, 0)
            gathers(1, 1, 0, 0)
            with pool.Fori(1, G_UNITS // 2) as i:
                gathers(2 * i, 0, 2 * i - 1, 1)
                gathers(2 * i + 1, 1, 2 * i, 0)
            gathers(None, 0, G_UNITS - 1, 1)

        @block.scalar
        def _(act):
            def rsqrt_seed(n, steps_at, slot=0):
                act.wait_ge(var_ready, n + 1)
                act.activation(lnv[:, slot:slot + 1], mean_var[:, slot, 1:2], ACT.Ln, bias=eps_col[:]).then_inc(act_step, 1)
                act.wait_ge(act_step, steps_at + 1)
                act.activation(rstd0[:, slot:slot + 1], lnv[:, slot:slot + 1], ACT.Exp, scale=-0.5).then_inc(rstd0_ready, 1)

            act.preload_act_table_set("natural_log_exp_and_others")
            for s in range(4):
                act.dma_start(w_ring[:, s], w_in_chunks[s]).then_inc(w_loaded[s], 16)
            act.dma_start(pool_w_sb[:], pool_w.rearrange("g c d -> c g d")).then_inc(small_loaded, 16)
            act.dma_start(pool_bs[:, 0, :], pool_b).then_inc(small_loaded, 16)
            act.dma_start(pool_bs[:, 1, :], pool_scale).then_inc(small_loaded, 16)
            act.dma_start(keys_sb[:], keys_t.rearrange("h c n -> c h n")).then_inc(small_loaded, 16)
            act.dma_start(wv, w_v.rearrange("(c p) n -> p c n", p=P)).then_inc(wv_loaded, 16)
            act.wait_ge(consts, 1)
            with act.Fori(0, BLOCKS // 2) as i:
                for par in range(2):
                    n = 2 * i + par
                    rsqrt_seed(n, n)
                    act.wait_ge(h0_transposed, n + 1)
                    act.activation(hT[:, :, cols(n)], bank[:, 4 + 2 * par:6 + 2 * par, :].rearrange("p b (c q) -> p (b c) q", q=P),
                                   ACT.Copy).then_inc(h0t_copied, 1)
            with act.Fori(0, 3) as kind:
                for s in range(4):
                    act.wait_ge(proj_done, 4 * kind + s + 1)
                    for half in range(2):
                        m = act.activation(uqk[:, bass.ds(4 * kind + s, 1), cols(half, HALF)].rearrange("p o t -> p (o t)"),
                                           bank[:, 4 * half + s, :], ACT.Copy, scale=kind_scale[:, bass.ds(kind, 1)])
                    m.then_inc(proj_copied, 1)
            for b in range(BLOCKS):
                act.wait_ge(v_done, b + 1)
                act.activation(v_all[:, b, :], bank[:, b, :], ACT.Copy).then_inc(v_copied, 1)

            def stage_queries(b, n):
                need(act, z_done, 2 * n)
                act.activation(q_pad[0:64, 0:HEADS:2, :], uqk[0:64, 4:8, cols(b)], ACT.Copy)
                act.activation(q_pad[64:128, 1:HEADS:2, :], uqk[64:128, 4:8, cols(b)], ACT.Copy).then_inc(q_staged, 1)

            def log_terms(n, c, steps_at, diagonal_of=None):
                hs = slice(c * PER_HALF, (c + 1) * PER_HALF)
                if diagonal_of is None:
                    act.wait_ge(z_done, 2 * n + c + 1)
                else:
                    act.wait_ge(z_capped, 2 * diagonal_of + c + 1)
                need(act, sp_ready, 2 * n + c - 1)
                act.activation(soft[:, hs], z[:, c, :].rearrange("p (h q) -> p h q", q=P), ACT.Abs).then_inc(act_step, 1)
                act.wait_ge(act_step, steps_at + 2 * c + 1)
                act.activation(soft[:, hs], soft[:, hs], ACT.Exp, scale=-1.0).then_inc(act_step, 1)
                act.wait_ge(act_step, steps_at + 2 * c + 2)
                act.activation(soft[:, hs], soft[:, hs], ACT.Ln, bias=one_col[:]).then_inc(ln_ready, 1)

            def weights(n, c):
                hs = slice(c * PER_HALF, (c + 1) * PER_HALF)
                act.wait_ge(c_done, 2 * n + c + 1)
                need(act, av_done, 2 * n + c - 1)
                act.activation(attn[:, hs], z[:, c, :].rearrange("p (h q) -> p h q", q=P), ACT.Exp).then_inc(a_ready, 1)

            def attention_out(b, n_end):
                act.wait_ge(av_done, 2 * n_end)
                act.activation(o_stage, o_ps, ACT.Copy).then_inc(o_copied, 1)

            def pooled_out(b):
                act.activation(mix_t[:, 0:4, :], uqk[:, 0:4, cols(b)], ACT.Copy).then_inc(mixp_staged, 1)

            def attention_transposed(b):
                act.wait_ge(o_transposed, b + 1)
                act.activation(mix_t[:, 4:8, :], oT_ps, ACT.Copy).then_inc(mix_copied, 1)

            def x1_transpose_out(b):
                act.wait_ge(x1_transposed, b + 1)
                act.activation(hT[:, :, cols(b)], xT_ps, ACT.Copy).then_inc(x1t_copied, 1)

            stage_queries(0, 0)
            act.wait_ge(pool_mixed, GROUPS)
            log_terms(0, 0, BLOCKS, 0)
            log_terms(0, 1, BLOCKS, 0)
            weights(0, 0)
            weights(0, 1)
            with act.Fori(1, BLOCKS) as b:
                first = first_step(act, b)
                steps_at = 4 * first + BLOCKS + b - 1
                attention_out(b - 1, first)
                stage_queries(b, first)
                attention_transposed(b - 1)
                pooled_out(b - 1)
                log_terms(first, 0, steps_at, b)
                log_terms(first, 1, steps_at, b)
                weights(first, 0)
                rsqrt_seed(BLOCKS + b - 1, 4 * first + BLOCKS + b + 3)
                with act.Fori(1, b + 1) as i:
                    n = act.snap(first + i)
                    log_terms(n, 0, 4 * n + BLOCKS + b)
                    weights(n - 1, 1)
                    log_terms(n, 1, 4 * n + BLOCKS + b)
                    weights(n, 0)
                weights(first + b, 1)
                x1_transpose_out(b - 1)
            attention_out(BLOCKS - 1, pairs_before(BLOCKS))
            pooled_out(BLOCKS - 1)
            attention_transposed(BLOCKS - 1)
            total = 4 * pairs_before(BLOCKS) + BLOCKS + BLOCKS - 1
            rsqrt_seed(2 * BLOCKS - 1, total)
            x1_transpose_out(BLOCKS - 1)
            def gate_exps(h, par):
                act.wait_ge(gate_in, h + 1)
                act.activation(best_s[par], best_s[par], ACT.Exp).then_inc(gate_exp, 1)

            def query_copies(i):
                for s in range(4):
                    act.wait_ge(wq_done, 4 * i + s + 1)
                    act.activation(qpeer[:, s % 2, :], bank[:, 2 * (s % 2):2 * (s % 2) + 2, :].rearrange("p b n -> p (b n)"),
                                   ACT.Copy).then_inc(qp_copied, 1)
                    if s % 2 and not (isinstance(i, int) and s == 1):
                        gate_exps(2 * i + s // 2 - 1, 1 - s // 2)

            peeled(act, 4, query_copies)
            gate_exps(PEER_HEADS - 1, 1)

            for r in range(3):
                act.wait_ge(picks_turned, r + 1)
                act.activation(pick_rows[:, r, :], bank[:, r, :], ACT.Copy).then_inc(picks_kept, 1)
            def gates_of_two_blocks(i):
                for slot in range(2):
                    need(act, gates_stored[slot], 32 * i)
                    for t in range(BLOCK_BATCHES):
                        act.wait_ge(gates_done, BLOCK_BATCHES * (2 * i + slot) + t + 1)
                        for kh in range(2):
                            m = act.activation(gates[slot][kh][:, :, t * BATCH:(t + 1) * BATCH],
                                               bank[:, 2 * (t % HOT_RING):2 * (t % HOT_RING) + 2, :].rearrange("p b (t n) -> p n (b t)", n=N_KEYS)[:, kh * KEY_HALF:(kh + 1) * KEY_HALF, :],
                                               ACT.Copy)
                        m.then_inc(gates_copied, 1)

            peeled(act, DENSE // 2, gates_of_two_blocks)
            act.wait_ge(x1_back, 16)
            for b in range(BLOCKS):
                act.activation(res[:, b, :], x1_all[:, b, :], ACT.Copy, scale=ALPHA).then_inc(res_init, 1)

            for par in range(2):
                act.wait_ge(gates_stored[par], 16 * DENSE)

            def load_u_tile(j, s):
                act.dma_start(ut_ring[:, s], u_tiles[bass.ds(j, 1)].rearrange("o p c e -> p (o c) e")).then_inc(ut_loaded[s], 16)

            def load_gate_tile(j, s):
                act.dma_start(g_ring[:, s, :], g_dram[bass.ds(j, 1)].rearrange("o p t -> p (o t)")).then_inc(gt_loaded[s], 16)

            for j in range(2):
                load_u_tile(j, j)
                load_gate_tile(j, j)
            act.sem_inc(hid_gelu, 2)

            def unit_gelu(n, par):
                act.wait_ge(u_free, U_RING + TOPK * (n + 1))
                act.wait_ge(act_ready, n + 1)
                act.activation(hid_g[:, par, :], hid[:, par, :], ACT.Gelu).then_inc(gelu_done, 1)

            def hidden_tiles(g, par, last=False):
                for q in range(TILE_GROUP):
                    j = TILE_GROUP * g + q
                    act.wait_ge(act_made, j + 1)
                    if not (last and q >= TILE_GROUP - 2):
                        load_gate_tile(j + 2, (q + 2) % 4)
                    act.wait_ge(hid_done, j + 1)
                    act.activation(gelu_ring[:, q % 2, :], bank[:, q % 2, :], ACT.Gelu).then_inc(hid_gelu, 1)
                    if not (last and q >= TILE_GROUP - 2):
                        load_u_tile(j + 2, q % 2)
                unit_gelu(g, par)

            def two_groups(i):
                for par in range(2):
                    hidden_tiles(2 * i + par, par)

            def out_seed(b, slot=0):
                rsqrt_seed(2 * BLOCKS + b, total + 1 + b, slot)

            pairs = PEER_HEADS // 2
            with act.Fori(0, pairs) as i:
                two_groups(i)
            with act.Fori(1, GATHERED - 1) as b:
                two_groups(pairs * b)
                out_seed(b - 1)
                with act.Fori(1, pairs) as i:
                    two_groups(pairs * b + i)
            two_groups(pairs * (GATHERED - 1))
            out_seed(GATHERED - 2)
            with act.Fori(pairs * (GATHERED - 1) + 1, pairs * GATHERED - 1) as i:
                two_groups(i)
            hidden_tiles(TILE_GROUPS - 2, 0)
            hidden_tiles(TILE_GROUPS - 1, 1, True)
            act.preload_act_table_set("natural_log_exp_and_others")
            for b in range(GATHERED - 1, BLOCKS):
                out_seed(b, b % 2)

        @block.tensor
        def _(pe):
            pe.wait_ge(consts, 1)
            def transpose_block(i, par):
                pe.wait_ge(h0_ready, 2 * i + par + 1)
                need(pe, h0t_copied, 2 * i + par - 1)
                for c in range(DCH):
                    mm = pe.transpose(bank[:, 4 + 2 * par + c // 4, cols(c % 4)], normed[:, par, cols(c)], ident[:])
                mm.then_inc(h0_transposed, 1)

            def project_chunk(s, half):
                for c in range(DCH):
                    mm = pe.matmul(bank[:, 4 * half + s, :], w_ring[:, s, c, :], hT[:, c, cols(half, HALF)],
                                   start=(c == 0), stop=(c == DCH - 1))
                return mm

            for n in range(BLOCKS // 2):
                transpose_block(n // 2, n % 2)
            for s in range(4):
                transpose_block((s + 4) // 2, s % 2)
                pe.wait_ge(h0t_copied, 4)
                pe.wait_ge(w_loaded[s], 16)
                project_chunk(s, 0)
            pe.wait_ge(h0t_copied, BLOCKS)
            for s in range(4):
                project_chunk(s, 1).then_inc(proj_done, 1)
            with pe.Fori(1, 3) as kind:
                for s in range(4):
                    pe.wait_ge(w_loaded[s], 16 * (kind + 1))
                    pe.wait_ge(proj_copied, 4 * kind + s - 3)
                    project_chunk(s, 0)
                    project_chunk(s, 1).then_inc(proj_done, 1)
            pe.wait_ge(wv_loaded, 16)
            pe.wait_ge(proj_copied, 12)
            for b in range(BLOCKS):
                for c in range(DCH):
                    mm = pe.matmul(bank[:, b, :], hT[:, c, cols(b)], wv[:, c, :], start=(c == 0), stop=(c == DCH - 1))
                mm.then_inc(v_done, 1)
            pe.wait_ge(small_loaded, 64)
            for g in range(GROUPS):
                pe.wait_ge(v_copied, 2 * g + 2)
                pe.wait_ge(pooled, g + 1)
                for half in range(2):
                    mm = pe.matmul(bank[:, 2 * g + half, :], pool_w_sb[:, g, :], uqk[:, g, cols(half, HALF)], start=True, stop=True)
                mm.then_inc(pool_mm, 1)
            pe.wait_ge(pool_mixed, GROUPS)

            def scores(n, c, diagonal_of=None):
                if c == 0:
                    pe.wait_ge(k_staged, n + 1)
                    if diagonal_of is not None:
                        pe.wait_ge(q_staged, diagonal_of + 1)
                need(pe, a_ready, 2 * n + c - 1)
                for hh in range(PER_HALF):
                    h = c * PER_HALF + hh
                    mm = pe.matmul(z[:, c, cols(hh)], k_stage[:, h // 2, :], q_pad[:, h, :], start=(hh == 0), stop=True, skip_group_check=True)
                mm.then_inc(z_done, 1)

            def sums(n, c, earlier=True):
                hs = slice(c * PER_HALF, (c + 1) * PER_HALF)
                pe.wait_ge(sp_ready, 2 * n + c + 1)
                mm = pe.matmul(z[:, c, :], neg_tri[:], sp[:, hs].rearrange("p h q -> p (h q)"), start=False, stop=True, skip_group_check=True)
                if earlier:
                    pe.wait_ge(sum_ready, 2 * n + c + 1)
                    mm = pe.matmul(z[:, c, :], neg_ones[:], sp_sum[:, hs].rearrange("p h q -> p (h q)"), start=False, stop=True, skip_group_check=True)
                mm.then_inc(c_done, 1)

            def values(n, c, key):
                pe.wait_ge(a_ready, 2 * n + c + 1)
                for hh in range(PER_HALF):
                    h = c * PER_HALF + hh
                    mm = pe.matmul(o_ps[:, cols(h, HEAD_DIM)], attn[:, h, :], v_all[:, bass.ds(key, 1), cols(h, HEAD_DIM)].rearrange("p o d -> p (o d)"),
                                   start=False, stop=True, skip_group_check=True)
                mm.then_inc(av_done, 1)

            def clear_values(b):
                need(pe, o_copied, b)
                pe.matmul(o_ps[:, 0:P], zero_row[:], ident[0:1, :], start=True, stop=True, skip_group_check=True)

            def attention_transposes(b):
                pe.wait_ge(o_copied, b + 1)
                for c in range(4):
                    mm = pe.transpose(oT_ps[:, c, :], o_stage[:, cols(c)], ident[:])
                mm.then_inc(o_transposed, 1)

            def output_projection(b):
                pe.wait_ge(mixp_staged, b + 1)
                pe.wait_ge(mix_copied, b + 1)
                need(pe, y_read, b)
                for half in range(2):
                    for c in range(DCH):
                        mm = pe.matmul(y_ps[:, cols(half, HALF)], mix_t[:, c, :], wo[:, c, cols(half, HALF)], start=(c == 0), stop=(c == DCH - 1))
                mm.then_inc(y_done, 1)

            def x1_transposes(b):
                pe.wait_ge(x1_ready, b + 1)
                need(pe, x1t_copied, b)
                for c in range(DCH):
                    mm = pe.transpose(xT_ps[:, c, :], normed[:, 0, cols(c)], ident[:])
                mm.then_inc(x1_transposed, 1)

            scores(0, 0, 0)
            scores(0, 1, 0)
            clear_values(0)
            sums(0, 0, False)
            sums(0, 1)
            values(0, 0, 0)
            values(0, 1, 0)
            pe.wait_ge(wo_loaded, 16)
            with pe.Fori(1, BLOCKS) as b:
                first = first_step(pe, b)
                attention_transposes(b - 1)
                scores(first, 0, b)
                scores(first, 1, b)
                output_projection(b - 1)
                clear_values(b)
                sums(first, 0, False)
                with pe.Fori(1, b + 1) as i:
                    n = pe.snap(first + i)
                    scores(n, 0)
                    sums(n - 1, 1)
                    values(n - 1, 0, key_block(b, i - 1))
                    scores(n, 1)
                    sums(n, 0)
                    values(n - 1, 1, key_block(b, i - 1))
                last = pe.snap(first + b)
                sums(last, 1)
                x1_transposes(b - 1)
                values(last, 0, 0)
                values(last, 1, 0)
            attention_transposes(BLOCKS - 1)
            output_projection(BLOCKS - 1)
            def queries(s, half):
                for c in range(DCH):
                    mm = pe.matmul(bank[:, 2 * (s % 2) + half, :], w_ring[:, s, c, :], hT[:, c, cols(half, HALF)],
                                   start=(c == 0), stop=(c == DCH - 1))
                return mm

            pe.wait_ge(x1t_copied, BLOCKS // 2)
            pe.wait_ge(w_loaded[0], 16 * 4)
            queries(0, 0)
            x1_transposes(BLOCKS - 1)
            pe.wait_ge(x1t_copied, BLOCKS)

            def query_chunks(i):
                for s in range(4):
                    par = s % 2
                    pe.wait_ge(w_loaded[s], 16 * (i + 4))
                    need(pe, qp_copied, 4 * i + s)
                    if not (isinstance(i, int) and s == 0):
                        queries(s, 0)
                    queries(s, 1).then_inc(wq_done, 1)
                    pe.wait_ge(qp_copied, 4 * i + s + 1)
                    pe.wait_ge(score_free, 4 * i + s + 1)
                    for b in range(BLOCKS):
                        mm = pe.matmul(bank[:, 4 + 2 * par + b // 4, cols(b % 4)], qpeer[:, par, cols(b)], keys_sb[:, s % 2, :], start=True, stop=True)
                    mm.then_inc(score_ready, 1)

            peeled(pe, 4, query_chunks)
            pe.wait_ge(picks_split, 1)
            pe.wait_ge(qp_copied, 16)
            for r in range(3):
                for b in range(DENSE):
                    mm = pe.transpose(bank[:, r, cols(b)], pick_cols[:, r, cols(b)], ident[:])
                mm.then_inc(picks_turned, 1)
            pe.wait_ge(picks_kept, 3)

            def gates_of_ring(i):
                for slot in range(HOT_RING):
                    n = HOT_RING * i + slot
                    pe.wait_ge(key1_gated, n + 1)
                    pe.wait_ge(key2_ready, n + 1)
                    need(pe, gates_copied, n - HOT_RING + 1)
                    for t in range(BATCH):
                        mm = pe.matmul(bank[:, 2 * slot + t // 4, cols(t % 4)], key2_hot[:, slot, t // 4, t % 4, :], key1_hot[:, slot, t // 4, t % 4, :],
                                       start=True, stop=True)
                    mm.then_inc(gates_done, 1)

            peeled(pe, BATCHES // HOT_RING, gates_of_ring)
            pe.wait_ge(gates_copied, BATCHES)
            pe.sem_inc(out_done, OUTS)

            def hidden_tile(g, q):
                j = TILE_GROUP * g + q
                pe.wait_ge(ut_loaded[q % 2], 16 * (2 * g + q // 2 + 1))
                pe.wait_ge(hid_gelu, j + 1)
                for c in range(DCH):
                    mm = pe.matmul(bank[:, q % 2, :], ut_ring[:, q % 2, c, :], hT[:, c, DT:SEQ], start=(c == 0), stop=(c == DCH - 1))
                mm.then_inc(hid_done, 1)

            def output_bank(g, par, o, vt_round):
                if o == 0:
                    pe.wait_ge(act_made, TILE_GROUP * (g + 1) + 2)
                    pe.wait_ge(vt_loaded[par], 16 * vt_round)
                pe.wait_ge(out_added, OUTS * g + o + 1)
                for q in range(TILE_GROUP):
                    s = TILE_GROUP * par + q
                    mm = pe.matmul(bank[:, 2 + o % OUT_RING, :], act_ring[:, s, cols(o // 2)], vt_ring[:, s, cols(o % 2, HALF)],
                                   start=(q == 0), stop=(q == TILE_GROUP - 1))
                mm.then_inc(out_done, 1)

            def group(g, par, vt_round):
                for q in range(TILE_GROUP):
                    hidden_tile(g, q)
                    if vt_round is None:
                        continue
                    for o in (2 * q, 2 * q + 1):
                        output_bank(g - 1, 1 - par, o, vt_round)

            group(0, 0, None)
            group(1, 1, 1)
            with pe.Fori(1, TILE_GROUPS // 2) as i:
                group(2 * i, 0, i)
                group(2 * i + 1, 1, i + 1)
            for o in range(OUTS):
                output_bank(TILE_GROUPS - 1, 1, o, TILE_GROUPS // 2)

        @block.vector
        def _(dve):
            def norm_stats(steps, src, slot=0):
                dve.bn_stats(stats[:, slot, 0, :], src[:, 0:HALF])
                steps.link(dve.bn_stats(stats[:, slot, 1, :], src[:, HALF:D]))
                dve.bn_aggr(mean_var[:, slot, :], stats[:, slot]).then_inc(var_ready, 1)

            def norm_apply(steps, n, src, dst, before_write, release=None, rows=ln_rows, slot=0):
                dve.wait_ge(var_ready, n + 1)
                before_write()
                m = dve.scalar_tensor_tensor(dst, src, mean_var[:, slot, 0:1], rows[:, 0, :], ALU.subtract, ALU.mult)
                if release is not None:
                    m.then_inc(release, 1)
                dve.wait_ge(rstd0_ready, n + 1)
                seed = rstd0[:, slot:slot + 1]
                steps.link(dve.tensor_tensor(newton[:], seed, seed, ALU.mult))
                steps.link(dve.scalar_tensor_tensor(newton[:], mean_var[:, slot, 1:2], LN_EPS, newton[:], ALU.add, ALU.mult))
                steps.link(dve.tensor_scalar(newton[:], newton[:], -0.5, 1.5, ALU.mult, ALU.add))
                steps.link(dve.tensor_tensor(rstd[:], seed, newton[:], ALU.mult))
                return dve.scalar_tensor_tensor(dst, dst, rstd[:], rows[:, 1, :], ALU.mult, ALU.add)

            def layer_norm(steps, n, src, dst, before_write, release=None):
                norm_stats(steps, src)
                return norm_apply(steps, n, src, dst, before_write, release)

            LN_LINKS = 5
            dve.wait_ge(consts, 1)
            steps = Steps(dve, dve_a, dve_passed)
            steps.link(dve.reciprocal(inv_count[:], inv_count[:]))
            dve.wait_ge(ln_loaded, 32)
            def norm_pair(i):
                steps.at(2 * LN_LINKS * i + 1)
                for par in range(2):
                    n = 2 * i + par
                    dve.wait_ge(x_loaded[par], 16 * (i + 1))

                    def slot_free():
                        need(dve, h0_transposed, 2 * i)
                        need(dve, h0_stored[par], 16 * i)

                    layer_norm(steps, n, xin[:, par, :], normed[:, par, :], slot_free, x_free).then_inc(h0_ready, 1)
                assert steps.k == 2 * LN_LINKS

            peeled(dve, BLOCKS // 2, norm_pair)
            steps = Steps(dve, dve_b)
            dve.wait_ge(small_loaded, 64)
            for g, w in enumerate(POOL_WINDOWS):
                dve.wait_ge(proj_copied, g + 1)
                u = uqk[:, g, :]
                cur, step = u, 1
                spare = [win_a, win_b]
                while step < w:
                    dst = spare.pop(0)
                    dve.tensor_tensor(dst[:, step:], cur[:, step:], cur[:, :SEQ - step], ALU.add)
                    steps.link(dve.tensor_copy(dst[:, :step], cur[:, :step]))
                    if cur is not u:
                        spare.append(cur)
                    cur, step = dst, 2 * step
                steps.link(dve.tensor_tensor(head_cols[:, :w - 1], cur[:, :w - 1], inv_count[:, :w - 1], ALU.mult))
                steps.link(dve.tensor_tensor(head_cols[:, :w - 1], head_cols[:, :w - 1], u[:, :w - 1], ALU.subtract))
                steps.link(dve.scalar_tensor_tensor(u, cur, 1.0 / w, u, ALU.mult, ALU.subtract))
                dve.tensor_copy(u[:, :w - 1], head_cols[:, :w - 1]).then_inc(pooled, 1)
            for g in range(GROUPS):
                dve.wait_ge(pool_mm, g + 1)
                dve.tensor_scalar(uqk[:, g, :], bank[:, 2 * g:2 * g + 2, :].rearrange("p b n -> p (b n)"),
                                  pool_bs[:, 0, g:g + 1], pool_bs[:, 1, g:g + 1], ALU.add, ALU.mult).then_inc(pool_mixed, 1)

            steps = Steps(dve, dve_c, dve_passed)

            def softplus(i, n):
                diagonal = isinstance(i, int) and i == 0
                if diagonal:
                    for c in range(HALVES):
                        zc = z[:, c, :].rearrange("p (h q) -> p h q", q=P)
                        dve.wait_ge(z_done, 2 * n + c + 1)
                        dve.tensor_tensor(zc, zc, cap[:].unsqueeze(1).broadcast_to([P, PER_HALF, P]), ALU.min).then_inc(z_capped, 1)
                for c in range(HALVES):
                    hs = slice(c * PER_HALF, (c + 1) * PER_HALF)
                    zc = z[:, c, :].rearrange("p (h q) -> p h q", q=P)
                    dve.wait_ge(ln_ready, 2 * n + c + 1)
                    need(dve, c_done, 2 * n + c - 1)
                    if not diagonal:
                        dve.wait_ge(sum_ready, 2 * n + c + 1)
                    dve.scalar_tensor_tensor(sp[:, hs], zc, 0.0, soft[:, hs], ALU.max, ALU.add).then_inc(sp_ready, 1)

            def norm_1(b):
                dve.wait_ge(h0_reloaded, 16 * (b + 1))
                dve.wait_ge(y_done, b + 1)
                dve.scalar_tensor_tensor(x1_pre, h0_back, ALPHA, y_ps, ALU.mult, ALU.add).then_inc(y_read, 1)
                dve.wait_ge(y_read, b + 1)

                def slot_free():
                    need(dve, x1_transposed, b)
                    need(dve, x1_stored, 16 * b)

                layer_norm(steps, BLOCKS + b, x1_pre, normed[:, 0, :], slot_free).then_inc(x1_ready, 1)

            softplus(0, 0)
            dve.wait_ge(ln_loaded, 64)
            dve.wait_ge(h0_transposed, BLOCKS)
            dve.wait_ge(h0_stored[0], 16 * (BLOCKS // 2))
            dve.wait_ge(h0_stored[1], 16 * (BLOCKS // 2))
            c_links = LN_LINKS
            with dve.Fori(1, BLOCKS) as b:
                steps.at(c_links * b - LN_LINKS)
                first = first_step(dve, b)
                softplus(0, first)
                norm_1(b - 1)
                assert steps.k == c_links
                with dve.Fori(1, b + 1) as i:
                    softplus(i, dve.snap(first + i))
            steps.at(c_links * BLOCKS - LN_LINKS)
            norm_1(BLOCKS - 1)

            steps = Steps(dve, dve_d, dve_passed)
            dve.sem_inc(score_free, 2)

            def top16(values, work, out_s, out_i, release=None):
                n = len(values)
                for j in range(n):
                    m = dve.max(out_s(j)[:, 0:8], values[j])
                steps.link(m)
                for j in range(n):
                    m = dve.max_index(out_i(j)[:, 0:8], out_s(j)[:, 0:8], values[j])
                for j in range(n):
                    m = dve.match_replace(work(j), out_s(j)[:, 0:8], values[j], LOWEST)
                steps.link(m)
                for j in range(n):
                    m = dve.max(out_s(j)[:, 8:16], work(j))
                steps.link(m)
                for j in range(n):
                    m = dve.max_index(out_i(j)[:, 8:16], out_s(j)[:, 8:16], work(j))
                steps.link(m)

            def finish_head(h, par):
                dve.wait_ge(match_weighed, h + 1)
                steps.link(dve.tensor_reduce(expert_f, match[par][:, :, 0:FOLDED], AX.X, ALU.add))
                idx_h = idx_all[:, 0:UNITS * TOPK].rearrange("p (b m) -> p b m", b=BLOCKS)[:, :, cols(h, TOPK)]
                gate_h = gate_all.rearrange("p (b m) -> p b m", b=BLOCKS)[:, :, cols(h, TOPK)]
                dve.tensor_copy(idx_h, expert_f.rearrange("p (b k) -> p b k", k=TOPK))
                dve.wait_ge(gate_exp, h + 1)
                steps.link(dve.tensor_reduce(gate_sum[:], best_s[par], AX.X, ALU.add))
                steps.link(dve.reciprocal(gate_sum[:], gate_sum[:]))
                steps.link(dve.tensor_tensor(gate_h, best_s[par], gate_sum[:].unsqueeze(2).broadcast_to([P, BLOCKS, TOPK]), ALU.mult))

            FINISH_LINKS = 4
            d_links = 2 * (2 * 4 + 4 + 4 + FINISH_LINKS)

            def head(h, par, first):
                for half in range(2):
                    dve.wait_ge(score_ready, 2 * h + half + 1)
                    dve.sem_inc(dve_passed, 1)
                    score = [bank[:, 4 + 2 * half + b // 4, cols(b % 4)] for b in range(BLOCKS)]
                    top16(score, lambda b: key_work[:, b, :], lambda b: top_s[:, half, b, :], lambda b: top_i[:, half, b, :])
                    dve.tensor_copy(top_if[:, half], top_i[:, half]).then_inc(score_free, 1)
                dve.wait_ge(score_free, 2 * h + 4)
                steps.link(dve.tensor_scalar(top_if[:, 0], top_if[:, 0], float(N_KEYS), None, ALU.mult))
                for lists, dst in ((top_s, cand), (top_if, cand_e[par])):
                    for a in range(5):
                        n = ROW_LEN[a]
                        m = dve.tensor_tensor(dst[:, :, ROW_AT[a]:ROW_AT[a] + n], lists[:, 1, :, 0:n],
                                              lists[:, 0, :, a:a + 1].broadcast_to([P, BLOCKS, n]), ALU.add)
                    m = dve.tensor_tensor(dst[:, :, ROW_AT[5]:ROW_AT[8]].rearrange("p b (a n) -> p b a n", n=2),
                                          lists[:, 1, :, 0:2].unsqueeze(2).broadcast_to([P, BLOCKS, 3, 2]),
                                          lists[:, 0, :, 5:8].unsqueeze(3).broadcast_to([P, BLOCKS, 3, 2]), ALU.add)
                    m = dve.tensor_tensor(dst[:, :, ROW_AT[8]:CANDS], lists[:, 0, :, 8:16],
                                          lists[:, 1, :, 0:1].broadcast_to([P, BLOCKS, 8]), ALU.add)
                steps.link(m)
                top16([cand[:, b, :] for b in range(BLOCKS)], lambda b: cand_w[:, b, :],
                      lambda b: best_s[par][:, b, :], lambda b: best_p[:, b, :])
                steps.link(dve.tensor_copy(best_pf, best_p))
                if not first:
                    finish_head(h - 1, 1 - par)
                flat_p = best_pf.rearrange("p b k -> p (b k)")
                dve.tensor_tensor(match[par], iota_k[:, 0:CANDS].unsqueeze(1).broadcast_to([P, BLOCKS * TOPK, CANDS]),
                                  flat_p.unsqueeze(2).broadcast_to([P, BLOCKS * TOPK, CANDS]), ALU.is_equal).then_inc(match_ready, 1)
                steps.link(dve.tensor_copy(gate_sum[:], best_s[par][:, :, 0]))
                dve.tensor_tensor(best_s[par], best_s[par], gate_sum[:].unsqueeze(2).broadcast_to([P, BLOCKS, TOPK]), ALU.subtract).then_inc(gate_in, 1)

            def head_pair(i):
                first = isinstance(i, int)
                if not first:
                    steps.at(d_links * i - FINISH_LINKS)
                head(2 * i, 0, first)
                head(2 * i + 1, 1, False)
                assert steps.k == d_links - FINISH_LINKS * first, steps.k

            peeled(dve, PEER_HEADS // 2, head_pair)
            steps.at(d_links * (PEER_HEADS // 2) - FINISH_LINKS)
            finish_head(PEER_HEADS - 1, 1)
            later = idx_all[:, GATHERED * PICKS:BLOCKS * PICKS]
            steps.link(dve.tensor_scalar(pick_cols[:, 0, :].bitcast(U32), later, 7, None, ALU.logical_shift_right))
            steps.link(dve.tensor_scalar(pick_cols[:, 1, :].bitcast(U32), later, N_KEYS - 1, None, ALU.bitwise_and))
            for r in range(2):
                steps.link(dve.tensor_copy(pick_cols[:, r, :], pick_cols[:, r, :].bitcast(U32)))
            dve.tensor_copy(pick_cols[:, 2, :], gate_all[:, GATHERED * PICKS:BLOCKS * PICKS]).then_inc(picks_split, 1)
            dve.wait_ge(picks_kept, 3)
            def hot_batch(t, par):
                for r, hot, ready in ((0, key1_hot, key1_ready), (1, key2_hot, key2_ready)):
                    dve.tensor_tensor(hot[:, par], iota_k[:].unsqueeze(1).unsqueeze(1).broadcast_to([P, BATCH // 4, 4, N_KEYS]),
                                      per_token(r, t), ALU.is_equal).then_inc(ready, 1)

            for slot in range(HOT_RING):
                hot_batch(slot, slot)
            with dve.Fori(1, BATCHES // HOT_RING) as i:
                for slot in range(HOT_RING):
                    dve.wait_ge(gates_done, HOT_RING * (i - 1) + slot + 1)
                    hot_batch(HOT_RING * i + slot, slot)
            dve.sem_inc(u_free, U_RING)
            dve.sem_inc(v_free, V_RING)
            dve.sem_inc(act_ready, 2)
            dve.sem_inc(act_made, 2)
            dve.sem_inc(out_added, OUT_RING)
            dve.wait_ge(x1_back, 16)
            dve.wait_ge(res_init, BLOCKS)
            dve.wait_ge(gates_done, BATCHES)
            dve.tensor_copy(idx_u[:, 0, :], idx_all[:, 0:TOPK]).then_inc(idx_u_staged, 1)

            def of_block(tokens, b):
                return tokens[:, bass.ds(b, 1), :].rearrange("p o d -> p (o d)")

            def weigh(n, par):
                dve.wait_ge(gelu_done, n + 1)
                dve.tensor_tensor(act_g[:, par, :], hid_g[:, par, :], gate_all[:, cols(n, TOPK)], ALU.mult).then_inc(act_ready, 1)
                dve.wait_ge(act_ready, n + 3)

            def dot(n, par, k, b):
                s = k % U_RING
                dve.wait_ge(u_loaded[s], 16 * (TOPK // U_RING * n + k // U_RING + 1))
                row = u_ring[:, s, :]
                dve.scalar_tensor_tensor(row, row, 1.0, of_block(x1_all, b), ALU.mult, ALU.mult,
                                         accum_out=hid[:, par, k:k + 1]).then_inc(u_free, 1)

            def add_row(n, par, k, b):
                s = k % V_RING
                dve.wait_ge(v_loaded[s], 16 * (TOPK // V_RING * n + k // V_RING + 1))
                dve.wait_ge(v_free, V_RING + TOPK * n + k)
                dve.scalar_tensor_tensor(of_block(res, b), v_ring[:, s, :], act_g[:, par, k:k + 1], of_block(res, b),
                                         ALU.mult, ALU.add).then_inc(v_free, 1)

            def gate_tile(g, par, q):
                dve.wait_ge(hid_gelu, TILE_GROUP * g + q + 3)
                dve.wait_ge(gt_loaded[q], 16 * (g + 1))
                if q == 0:
                    need(dve, out_done, OUTS * g)
                dve.tensor_tensor(act_ring[:, TILE_GROUP * par + q, :], gelu_ring[:, q % 2, :], g_ring[:, q, :], ALU.mult).then_inc(act_made, 1)

            def add_output(g, o):
                dve.wait_ge(out_done, OUTS * (g + 1) + o + 1)
                r = res[:, GATHERED + o // 2, cols(o % 2, HALF)]
                dve.tensor_tensor(r, r, bank[:, 2 + o % OUT_RING, :], ALU.add).then_inc(out_added, 1)

            def unit(n, par, b, b_before, first=False):
                if not first:
                    dve.wait_ge(out_added, OUTS * (n - 1) + OUT_RING)
                for k in range(TOPK):
                    dot(n, par, k, b)
                    if k == 1 and not first:
                        weigh(n - 1, 1 - par)
                    if k >= 1 and not first:
                        add_row(n - 1, 1 - par, k - 1, b_before)
                    if k == 3:
                        dve.tensor_copy(idx_v[:, par, :], idx_all[:, cols(n, TOPK)]).then_inc(idx_v_staged, 1)
                        dve.tensor_copy(idx_u[:, 1 - par, :], idx_all[:, cols(n + 1, TOPK)]).then_inc(idx_u_staged, 1)
                    if k % 4 == 3:
                        gate_tile(n, par, k // 4)
                        if not first:
                            for o in (k // 4 * 2, k // 4 * 2 + 1):
                                add_output(n - 1, o)
                if not first:
                    add_row(n - 1, 1 - par, TOPK - 1, b_before)

            def unit_pair(i, b, b_before):
                unit(2 * i, 0, b, b_before)
                unit(2 * i + 1, 1, b, b)

            norm_steps = Steps(dve, dve_e, dve_passed)

            def norm_out(b):
                norm_steps.at(LN_LINKS * b)
                r = of_block(res, b)
                norm_stats(norm_steps, r)
                norm_apply(norm_steps, 2 * BLOCKS + b, r, r, lambda: None, rows=ln2_rows).then_inc(out_ready, 1)

            pairs = PEER_HEADS // 2
            dve.wait_ge(ln_loaded, 96)
            unit(0, 0, 0, 0, True)
            unit(1, 1, 0, 0)
            with dve.Fori(1, pairs) as i:
                unit_pair(i, 0, 0)
            with dve.Fori(1, GATHERED) as b:
                unit_pair(pairs * b, b, b - 1)
                norm_out(b - 1)
                with dve.Fori(1, pairs) as i:
                    unit_pair(pairs * b + i, b, b)
            weigh(G_UNITS - 1, 1)
            dve.wait_ge(out_added, OUTS * (TILE_GROUPS - 1) + OUT_RING)
            for k in range(TOPK):
                add_row(G_UNITS - 1, 1, k, GATHERED - 1)
                if k % 2:
                    add_output(TILE_GROUPS - 1, k // 2)
            dve.wait_ge(v_free, V_RING + TOPK * G_UNITS)
            dve.wait_ge(out_added, OUTS * TILE_GROUPS + OUT_RING)
            steps = norm_steps
            steps.at(LN_LINKS * (GATHERED - 1))
            norm_stats(steps, res[:, GATHERED - 1, :], (GATHERED - 1) % 2)
            for b in range(GATHERED - 1, BLOCKS):
                if b + 1 < BLOCKS:
                    norm_stats(steps, res[:, b + 1, :], (b + 1) % 2)
                norm_apply(steps, 2 * BLOCKS + b, res[:, b, :], res[:, b, :], lambda: None,
                           rows=ln2_rows, slot=b % 2).then_inc(out_ready, 1)


def kernel(**inputs):
    import numpy as _np
    import concourse.bacc as _bacc
    from concourse import mybir as _mybir
    from concourse.bass_utils import run_bass_kernel_spmd as _run

    a = {k: _np.asarray(v) for k, v in inputs.items()}
    w_in = a["w_in"][0]
    laid = {
        "x": a["x"].reshape(SEQ, D),
        "ln0_g": a["ln0_g"], "ln0_b": a["ln0_b"],
        "w_in_chunks": w_in[:, :12 * P].reshape(DCH, P, 12, P).transpose(2, 1, 0, 3),
        "w_v": w_in[:, 12 * P:],
        "pool_w": a["pool_w"][0],
        "pool_b": a["pool_b"][0].T,
        "pool_scale": a["pool_scale"][0].reshape(GROUPS, P).T,
        "w_out": a["w_out"][0],
        "ln1_g": a["ln1_g"][0], "ln1_b": a["ln1_b"][0],
        "wq_chunks": a["peer_wq"][0].reshape(DCH, P, 16, P).transpose(2, 1, 0, 3),
        "keys_t": a["peer_sub_keys"][0].transpose(0, 2, 1),
        "peer_u": a["peer_u"][0], "peer_v": a["peer_v"][0],
        "u_tiles": a["peer_u"][0].reshape(TILES, P, DCH, P).transpose(0, 3, 2, 1),
        "ln2_g": a["ln2_g"][0], "ln2_b": a["ln2_b"][0],
    }
    nc = _bacc.Bacc("TRN2", target_bir_lowering=False, num_devices=1)
    arrays, args = {}, []
    for name, v in laid.items():
        v = _np.ascontiguousarray(v)
        arrays[f"in_{name}"] = v
        args.append(nc.dram_tensor(f"in_{name}", v.shape, _mybir.dt.from_np(v.dtype), kind="ExternalInput").ap())
    o = nc.dram_tensor("out_0", (SEQ, D), F32, kind="ExternalOutput").ap()
    layer_kernel(nc, *args, o)
    r = _run(nc, [arrays], core_ids=[0])
    return r.results[0]["out_0"].reshape(a["x"].shape)
```
